# Optimizing a Trainium2 kernel written in Bass

```python
import math
import jax, jax.numpy as jnp
from jax import lax
import numpy as np

D_MODEL = 1024
BATCH = 1
SEQ = 256
DEPTH = 2

N_A = DEPTH // 2
N_B = DEPTH - N_A
CONV_WIDTH = 31
N_HEADS = 8
HEAD_DIM = 64
V_DIM = 2 * HEAD_DIM
QK_WIDTH = 2 * N_HEADS * HEAD_DIM
V_WIDTH = N_HEADS * V_DIM
N_BUCKETS = 32
MAX_DISTANCE = 128
Q_BLOCK = 128
N_EXPERTS = 16
N_GROUPS = 4
EXPERTS_PER_GROUP = N_EXPERTS // N_GROUPS
TOP_K = 2
D_EXPERT = 512
ALPHA = (2.0 * DEPTH) ** 0.25
BETA = (8.0 * DEPTH) ** -0.25
LN_EPS = 1e-5


def layer_norm(x, g, b):
    xf = x.astype(jnp.float32)
    mu = jnp.mean(xf, -1, keepdims=True)
    var = jnp.mean(jnp.square(xf - mu), -1, keepdims=True)
    return ((xf - mu) * lax.rsqrt(var + LN_EPS) * g.astype(jnp.float32) + b.astype(jnp.float32)).astype(x.dtype)

def conformer_conv(x, w_pw1, b_pw1, w_dw, b_dw, g, b, w_pw2, b_pw2):
    h = x @ w_pw1 + b_pw1
    a, gate = jnp.split(h, 2, axis=-1)
    h = a * jax.nn.sigmoid(gate)
    h = lax.conv_general_dilated(
        h, w_dw[:, None, :].astype(h.dtype), window_strides=(1,),
        padding=[(CONV_WIDTH - 1, 0)],
        dimension_numbers=("NWC", "WIO", "NWC"),
        feature_group_count=D_MODEL) + b_dw
    h = jax.nn.silu(layer_norm(h, g, b))
    return h @ w_pw2 + b_pw2

def t5_bucket(n):
    n = jnp.maximum(n, 0)
    max_exact = N_BUCKETS // 2
    nf = jnp.maximum(n, 1).astype(jnp.float32)
    large = max_exact + (jnp.log(nf / max_exact) / math.log(MAX_DISTANCE / max_exact)
                         * (N_BUCKETS - max_exact)).astype(jnp.int32)
    large = jnp.minimum(large, N_BUCKETS - 1)
    return jnp.where(n < max_exact, n, large)

def diff_attention(x, k1, k2, v, w_q, lam_params, subln_g, w_o, rel_bias, layer_idx):
    bsz, seq, _ = x.shape
    n_blk = seq // Q_BLOCK
    lambda_init = 0.8 - 0.6 * math.exp(-0.3 * layer_idx)
    lp = lam_params.astype(jnp.float32)
    lam = jnp.exp(jnp.sum(lp[0] * lp[1])) - jnp.exp(jnp.sum(lp[2] * lp[3])) + lambda_init
    q = (x @ w_q).reshape(bsz, n_blk, Q_BLOCK, 2, N_HEADS, HEAD_DIM)
    q = jnp.transpose(q, (3, 1, 0, 4, 2, 5))
    scale = HEAD_DIM ** -0.5
    k_pos = jnp.arange(seq)

    def block(args):
        qb1, qb2, i = args
        q_pos = i * Q_BLOCK + jnp.arange(Q_BLOCK)
        rel = q_pos[:, None] - k_pos[None, :]
        bias = jnp.transpose(jnp.take(rel_bias, t5_bucket(rel), axis=0), (2, 0, 1)).astype(jnp.float32)
        causal = rel >= 0

        def probs(qb, k):
            s = jnp.einsum("bhqd,bhkd->bhqk", qb, k).astype(jnp.float32) * scale + bias
            return jax.nn.softmax(jnp.where(causal, s, -jnp.inf), axis=-1)

        a = probs(qb1, k1) - lam * probs(qb2, k2)
        return jnp.einsum("bhqk,bhkv->bhqv", a.astype(v.dtype), v)

    out = lax.map(block, (q[0], q[1], jnp.arange(n_blk)))
    out = jnp.transpose(out, (1, 0, 3, 2, 4)).reshape(bsz, seq, N_HEADS, V_DIM)
    of = out.astype(jnp.float32)
    of = of * lax.rsqrt(jnp.mean(jnp.square(of), -1, keepdims=True) + LN_EPS) * subln_g.astype(jnp.float32)
    of = of * (1.0 - lambda_init)
    return of.astype(x.dtype).reshape(bsz, seq, V_WIDTH) @ w_o

def grouped_moe(x, router_w, router_bias, w_gate, w_up, w_down):
    bsz, seq, d = x.shape
    x2 = x.reshape(-1, d)
    aff = jax.nn.sigmoid((x2 @ router_w).astype(jnp.float32))
    sel = (aff + router_bias.astype(jnp.float32)).reshape(-1, N_GROUPS, EXPERTS_PER_GROUP)
    grp_score = jnp.sum(lax.top_k(sel, 2)[0], -1)
    g_idx = jnp.argmax(grp_score, -1)
    in_grp = jnp.take_along_axis(sel, g_idx[:, None, None], axis=1)[:, 0]
    _, local = lax.top_k(in_grp, TOP_K)
    e_idx = g_idx[:, None] * EXPERTS_PER_GROUP + local
    w = jnp.take_along_axis(aff, e_idx, -1)
    w = w / jnp.sum(w, -1, keepdims=True)
    gates = jnp.sum(jax.nn.one_hot(e_idx, N_EXPERTS, dtype=jnp.float32) * w[..., None], axis=1)

    def step(acc, ew):
        g_e, wg_e, wu_e, wd_e = ew
        h = jax.nn.silu(x2 @ wg_e) * (x2 @ wu_e)
        return acc + (h @ wd_e) * g_e[:, None].astype(x2.dtype), None

    out, _ = lax.scan(step, jnp.zeros_like(x2), (gates.T, w_gate, w_up, w_down))
    return out.reshape(bsz, seq, d)

def first_inputs(seed: int = 0) -> dict:
    key = jax.random.key(seed)
    ks = jax.random.split(key, 32)
    nrm = jax.random.normal
    D, f32 = D_MODEL, jnp.float32
    w_kv_k = nrm(ks[9], (D, QK_WIDTH), f32) * D ** -0.5
    w_kv_v = nrm(ks[10], (D, V_WIDTH), f32) * D ** -0.5 * BETA
    return {
        "x": nrm(ks[0], (BATCH, SEQ, D), f32),
        "a_w_pw1": nrm(ks[1], (N_A, D, 2 * D), f32) * D ** -0.5,
        "a_b_pw1": 0.02 * nrm(ks[2], (N_A, 2 * D), f32),
        "a_w_dw": nrm(ks[3], (N_A, CONV_WIDTH, D), f32) * CONV_WIDTH ** -0.5,
        "a_b_dw": 0.02 * nrm(ks[4], (N_A, D), f32),
        "a_ln_g": 1.0 + 0.02 * nrm(ks[5], (N_A, D), f32),
        "a_ln_b": 0.02 * nrm(ks[6], (N_A, D), f32),
        "a_w_pw2": nrm(ks[7], (N_A, D, D), f32) * D ** -0.5 * BETA,
        "a_b_pw2": 0.02 * nrm(ks[8], (N_A, D), f32),
        "w_kv": jnp.concatenate([w_kv_k, w_kv_v], axis=1),
        "b_w_q": nrm(ks[11], (N_B, D, QK_WIDTH), f32) * D ** -0.5,
        "b_lambda": 0.1 * nrm(ks[12], (N_B, 4, HEAD_DIM), f32),
        "b_subln_g": 1.0 + 0.02 * nrm(ks[13], (N_B, V_DIM), f32),
        "b_w_o": nrm(ks[14], (N_B, V_WIDTH, D), f32) * V_WIDTH ** -0.5 * BETA,
        "rel_bias": 0.5 * nrm(ks[15], (N_BUCKETS, N_HEADS), f32),
        "ln_mix_g": 1.0 + 0.02 * nrm(ks[16], (DEPTH, D), f32),
        "ln_mix_b": 0.02 * nrm(ks[17], (DEPTH, D), f32),
        "ln_ffn_g": 1.0 + 0.02 * nrm(ks[18], (DEPTH, D), f32),
        "ln_ffn_b": 0.02 * nrm(ks[19], (DEPTH, D), f32),
        "router_w": nrm(ks[20], (D, N_EXPERTS), f32) * D ** -0.5,
        "router_bias": 0.01 * nrm(ks[21], (N_EXPERTS,), f32),
        "moe_w_gate": nrm(ks[22], (DEPTH, N_EXPERTS, D, D_EXPERT), f32) * D ** -0.5,
        "moe_w_up": nrm(ks[23], (DEPTH, N_EXPERTS, D, D_EXPERT), f32) * D ** -0.5,
        "moe_w_down": nrm(ks[24], (DEPTH, N_EXPERTS, D_EXPERT, D), f32) * D_EXPERT ** -0.5 * BETA,
    }

def first_block(x, a_w_pw1, a_b_pw1, a_w_dw, a_b_dw, a_ln_g, a_ln_b, a_w_pw2, a_b_pw2,
              w_kv, b_w_q, b_lambda, b_subln_g, b_w_o, rel_bias,
              ln_mix_g, ln_mix_b, ln_ffn_g, ln_ffn_b,
              router_w, router_bias, moe_w_gate, moe_w_up, moe_w_down):
    bsz, seq, _ = x.shape
    k1 = k2 = v = None
    for l in range(DEPTH):
        if l < N_A:
            mix = conformer_conv(x, a_w_pw1[l], a_b_pw1[l], a_w_dw[l], a_b_dw[l],
                                 a_ln_g[l], a_ln_b[l], a_w_pw2[l], a_b_pw2[l])
        else:
            if l == N_A:
                kv = x @ w_kv
                k = kv[..., :QK_WIDTH].reshape(bsz, seq, 2, N_HEADS, HEAD_DIM)
                k = jnp.transpose(k, (2, 0, 3, 1, 4))
                k1, k2 = k[0], k[1]
                v = jnp.transpose(kv[..., QK_WIDTH:].reshape(bsz, seq, N_HEADS, V_DIM), (0, 2, 1, 3))
            j = l - N_A
            mix = diff_attention(x, k1, k2, v, b_w_q[j], b_lambda[j], b_subln_g[j], b_w_o[j], rel_bias, l)
        x = layer_norm(ALPHA * x + mix, ln_mix_g[l], ln_mix_b[l])
        ffn = grouped_moe(x, router_w, router_bias, moe_w_gate[l], moe_w_up[l], moe_w_down[l])
        x = layer_norm(ALPHA * x + ffn, ln_ffn_g[l], ln_ffn_b[l])
    return x


DEPTH_2 = 1

ATTN_HEADS = 8
ATTN_KV_GROUPS = 2
IDX_HEADS = 4
IDX_DIM = 64
TOPK_MAX = 256
NUM_BUCKETS = 32
HGRN_HEADS = 4
HGRN_DIM = 128
HGRN_CHUNK = 64
CONV_W = 512
CONV_K = 3
D_FF = 4 * D_MODEL

ATTN_W = ATTN_HEADS * HEAD_DIM
KV_W = ATTN_KV_GROUPS * HEAD_DIM
HGRN_W = HGRN_HEADS * HGRN_DIM
N_BRANCH = 3
EPS = 1e-6
SPLITS = (ATTN_W, KV_W, KV_W,
          IDX_HEADS * IDX_DIM, IDX_DIM, IDX_HEADS,
          HGRN_W, HGRN_W, HGRN_W, HGRN_W,
          CONV_W, CONV_W, CONV_W,
          N_BRANCH * D_MODEL)
D_IN_PROJ = sum(SPLITS)


def _rmsnorm(x, g):
    xf = x.astype(jnp.float32)
    y = xf * lax.rsqrt(jnp.mean(xf * xf, axis=-1, keepdims=True) + EPS)
    return (y * g.astype(jnp.float32)).astype(x.dtype)

def _split_cols(p):
    offs, acc = [], 0
    for w in SPLITS[:-1]:
        acc += w
        offs.append(acc)
    return jnp.split(p, offs, axis=-1)

def _t5_bucket(dist):
    max_exact = NUM_BUCKETS // 2
    d = jnp.maximum(dist, 0)
    df = jnp.maximum(d, 1).astype(jnp.float32)
    large = max_exact + (jnp.log(df / max_exact) / math.log(MAX_DISTANCE / max_exact)
                         * (NUM_BUCKETS - max_exact)).astype(jnp.int32)
    large = jnp.minimum(large, NUM_BUCKETS - 1)
    return jnp.where(d < max_exact, d, large)

def _dsa_attention(q, k, v, qi, ki, wi, rel_bias):
    b, s = q.shape[0], q.shape[1]
    n_sel = min(TOPK_MAX, s // 4)
    nb = s // Q_BLOCK
    npg = ATTN_HEADS // ATTN_KV_GROUPS
    scale = HEAD_DIM ** -0.5
    wi = wi * (IDX_HEADS ** -0.5 * IDX_DIM ** -0.5)
    key_pos = jnp.arange(s)
    bidx = jnp.arange(b)[:, None, None]

    def blocks(a):
        return jnp.moveaxis(a.reshape((b, nb, Q_BLOCK) + a.shape[2:]), 1, 0)

    def one_block(args):
        blk, q_b, qi_b, wi_b = args
        t = blk * Q_BLOCK + jnp.arange(Q_BLOCK)
        sc = jax.nn.relu(jnp.einsum('bqhd,bsd->bqhs', qi_b, ki))
        sc = jnp.einsum('bqhs,bqh->bqs', sc, wi_b).astype(jnp.float32)
        causal = key_pos[None, :] <= t[:, None]
        sc = jnp.where(causal[None], sc, -jnp.inf)
        _, idx = lax.top_k(sc, n_sel)
        valid = idx <= t[None, :, None]
        k_sel = k[bidx, idx]
        v_sel = v[bidx, idx]
        qg = q_b.reshape(b, Q_BLOCK, ATTN_KV_GROUPS, npg, HEAD_DIM)
        logits = jnp.einsum('bqgnd,bqkgd->bqgnk', qg, k_sel).astype(jnp.float32) * scale
        bias = rel_bias[_t5_bucket(t[None, :, None] - idx)]
        bias = jnp.moveaxis(bias, -1, 2).reshape(b, Q_BLOCK, ATTN_KV_GROUPS, npg, n_sel)
        logits = jnp.where(valid[:, :, None, None, :], logits + bias.astype(jnp.float32), -jnp.inf)
        p = jax.nn.softmax(logits, axis=-1).astype(v.dtype)
        o = jnp.einsum('bqgnk,bqkgd->bqgnd', p, v_sel)
        return o.reshape(b, Q_BLOCK, ATTN_W)

    out = lax.map(one_block, (jnp.arange(nb), blocks(q), blocks(qi), blocks(wi)))
    return jnp.moveaxis(out, 0, 1).reshape(b, s, ATTN_W)

def _hgrn2(q, f_logit, i, lb):
    b, s = q.shape[0], q.shape[1]
    nc = s // HGRN_CHUNK
    f32 = jnp.float32
    z = f_logit.astype(f32)
    lb = lb.astype(f32).reshape(HGRN_HEADS, HGRN_DIM)
    log_f = jnp.logaddexp(jnp.log(lb), jnp.log1p(-lb) + jax.nn.log_sigmoid(z))
    kk = (1.0 - lb) * jax.nn.sigmoid(-z)

    def chunks(a):
        return a.reshape(b, nc, HGRN_CHUNK, HGRN_HEADS, HGRN_DIM).transpose(1, 0, 3, 2, 4)

    tri = jnp.tril(jnp.ones((HGRN_CHUNK, HGRN_CHUNK), dtype=bool))

    def step(state, inp):
        qc, kc, ic, gc = inp
        G = jnp.cumsum(gc, axis=2)
        diff = G[:, :, :, None, :] - G[:, :, None, :, :]
        decay = jnp.exp(jnp.where(tri[:, :, None], diff, -jnp.inf))
        attn = jnp.einsum('bhtd,bhsd,bhtsd->bhts', qc, kc, decay)
        o = attn @ ic + jnp.einsum('bhtd,bhdv->bhtv', qc * jnp.exp(G), state)
        g_last = G[:, :, -1:, :]
        state = (jnp.exp(g_last[:, :, 0, :, None]) * state
                 + jnp.einsum('bhsd,bhsv->bhdv', kc * jnp.exp(g_last - G), ic))
        return state, o

    s0 = jnp.zeros((b, HGRN_HEADS, HGRN_DIM, HGRN_DIM), f32)
    _, o = lax.scan(step, s0, (chunks(q.astype(f32)), chunks(kk), chunks(i.astype(f32)), chunks(log_f)))
    return o.transpose(1, 0, 3, 2, 4).reshape(b, s, HGRN_HEADS, HGRN_DIM)

def _short_conv(u, w):
    kern = w[:, None, :].astype(u.dtype)
    return lax.conv_general_dilated(u, kern, (1,), [(CONV_K - 1, 0)],
                                    dimension_numbers=('NWC', 'WIO', 'NWC'),
                                    feature_group_count=u.shape[-1])

def second_inputs(seed: int = 0) -> dict:
    key = jax.random.key(seed)
    ks = jax.random.split(key, 16)
    f32 = jnp.float32

    def nrm(k, shape, scale):
        return jax.random.normal(k, shape, f32) * scale

    def gain(k, shape):
        return 1.0 + 0.02 * jax.random.normal(k, shape, f32)

    return {
        'x': nrm(ks[0], (BATCH, SEQ, D_MODEL), 1.0),
        'rel_bias': nrm(ks[1], (NUM_BUCKETS, ATTN_HEADS), 0.5),
        'hgrn_lb': nrm(ks[2], (DEPTH_2, HGRN_W), 1.0),
        'ln_mix_g': gain(ks[3], (DEPTH_2, D_MODEL)),
        'w_in': nrm(ks[4], (DEPTH_2, D_MODEL, D_IN_PROJ), D_MODEL ** -0.5),
        'q_norm_g': gain(ks[5], (DEPTH_2, HEAD_DIM)),
        'k_norm_g': gain(ks[6], (DEPTH_2, HEAD_DIM)),
        'hgrn_norm_g': gain(ks[7], (DEPTH_2, HGRN_DIM)),
        'conv_w': nrm(ks[8], (DEPTH_2, CONV_K, CONV_W), CONV_K ** -0.5),
        'w_up_attn': nrm(ks[9], (DEPTH_2, ATTN_W, D_MODEL), ATTN_W ** -0.5),
        'w_up_hgrn': nrm(ks[10], (DEPTH_2, HGRN_W, D_MODEL), HGRN_W ** -0.5),
        'w_up_conv': nrm(ks[11], (DEPTH_2, CONV_W, D_MODEL), CONV_W ** -0.5),
        'w_out': nrm(ks[12], (DEPTH_2, D_MODEL, D_MODEL), D_MODEL ** -0.5),
        'ln_mlp_g': gain(ks[13], (DEPTH_2, D_MODEL)),
        'w_mlp_up': nrm(ks[14], (DEPTH_2, D_MODEL, D_FF), D_MODEL ** -0.5),
        'w_mlp_down': nrm(ks[15], (DEPTH_2, D_FF, D_MODEL), D_FF ** -0.5),
    }

def second_block(x, rel_bias, hgrn_lb, ln_mix_g, w_in, q_norm_g, k_norm_g, hgrn_norm_g,
              conv_w, w_up_attn, w_up_hgrn, w_up_conv, w_out, ln_mlp_g, w_mlp_up, w_mlp_down):
    b, s, _ = x.shape
    lb_all = jnp.cumsum(jax.nn.softmax(hgrn_lb.astype(jnp.float32), axis=0), axis=0)
    lb_all = lb_all - lb_all[0]
    for l in range(DEPTH_2):
        h = _rmsnorm(x, ln_mix_g[l])
        proj = h @ w_in[l]
        (aq, ak, av, iq, ik, iw, hq, hf, hi, hg, cb, cc, ch, gates) = _split_cols(proj)
        q = _rmsnorm(aq.reshape(b, s, ATTN_HEADS, HEAD_DIM), q_norm_g[l])
        k = _rmsnorm(ak.reshape(b, s, ATTN_KV_GROUPS, HEAD_DIM), k_norm_g[l])
        v = av.reshape(b, s, ATTN_KV_GROUPS, HEAD_DIM)
        y_attn = _dsa_attention(q, k, v, iq.reshape(b, s, IDX_HEADS, IDX_DIM), ik, iw, rel_bias)
        o = _hgrn2(hq.reshape(b, s, HGRN_HEADS, HGRN_DIM), hf.reshape(b, s, HGRN_HEADS, HGRN_DIM),
                   hi.reshape(b, s, HGRN_HEADS, HGRN_DIM), lb_all[l])
        y_hgrn = (_rmsnorm(o, hgrn_norm_g[l]).astype(x.dtype)
                  * jax.nn.silu(hg.reshape(b, s, HGRN_HEADS, HGRN_DIM))).reshape(b, s, HGRN_W)
        y_conv = cb * _short_conv(cc * ch, conv_w[l])
        g = jax.nn.sigmoid(gates.reshape(b, s, N_BRANCH, D_MODEL))
        mixed = (g[:, :, 0] * (y_attn @ w_up_attn[l])
                 + g[:, :, 1] * (y_hgrn @ w_up_hgrn[l])
                 + g[:, :, 2] * (y_conv @ w_up_conv[l]))
        x = x + mixed @ w_out[l]
        h = _rmsnorm(x, ln_mlp_g[l])
        x = x + jnp.square(jax.nn.relu(h @ w_mlp_up[l])) @ w_mlp_down[l]
    return x


def setup_inputs(seed=0):
    out = dict(first_inputs(seed))
    for name, value in second_inputs(seed + 1).items():
        if name != "x":
            out[name + "_2"] = value
    return out


def reference(
    x, a_w_pw1, a_b_pw1, a_w_dw, a_b_dw, a_ln_g, a_ln_b, a_w_pw2, a_b_pw2, w_kv, b_w_q,
    b_lambda, b_subln_g, b_w_o, rel_bias, ln_mix_g, ln_mix_b, ln_ffn_g, ln_ffn_b, router_w,
    router_bias, moe_w_gate, moe_w_up, moe_w_down, rel_bias_2, hgrn_lb_2, ln_mix_g_2, w_in_2,
    q_norm_g_2, k_norm_g_2, hgrn_norm_g_2, conv_w_2, w_up_attn_2, w_up_hgrn_2, w_up_conv_2,
    w_out_2, ln_mlp_g_2, w_mlp_up_2, w_mlp_down_2,
):
    x = first_block(
        x, a_w_pw1, a_b_pw1, a_w_dw, a_b_dw, a_ln_g, a_ln_b, a_w_pw2, a_b_pw2, w_kv, b_w_q,
        b_lambda, b_subln_g, b_w_o, rel_bias, ln_mix_g, ln_mix_b, ln_ffn_g, ln_ffn_b, router_w,
        router_bias, moe_w_gate, moe_w_up, moe_w_down,
    )
    return second_block(
        x, rel_bias_2, hgrn_lb_2, ln_mix_g_2, w_in_2, q_norm_g_2, k_norm_g_2, hgrn_norm_g_2,
        conv_w_2, w_up_attn_2, w_up_hgrn_2, w_up_conv_2, w_out_2, ln_mlp_g_2, w_mlp_up_2,
        w_mlp_down_2,
    )


_drawn_inputs = setup_inputs


def setup_inputs(seed=0):
    import zlib

    import numpy as np

    out = dict(_drawn_inputs(seed))
    spreads = {}
    factors = {'b_subln_g': 2.743,
     'q_norm_g_2': 8.0,
     'k_norm_g_2': 8.0,
     'hgrn_norm_g_2': 8.0,
     'ln_mlp_g_2': 3.355}
    for name, (base, spread) in spreads.items():
        noise = np.random.default_rng([zlib.crc32(name.encode()), seed]).standard_normal(out[name].shape)
        drawn = base * np.exp(spread * noise) if base else spread * noise
        out[name] = __import__('jax').numpy.asarray(drawn.astype(out[name].dtype))
    for name, factor in factors.items():
        out[name] = (out[name] * factor).astype(out[name].dtype)
    return out
```

```python
from contextlib import ExitStack
import math

import concourse.bass as bass
from concourse import mybir

F32 = mybir.dt.float32
I32 = mybir.dt.int32
ALU = mybir.AluOpType
ACT = mybir.ActivationFunctionType
AX = mybir.AxisListType.X

P = 128
D = 1024
T = 256
NT = T // P
KD = D // P
HALF = 512
RING = 4
BLK = 4096
LAYERS = 2
CONV = 31
DVE_CHUNKS = ((0, 1, 2), (3, 4))
PE_CHUNKS = (5, 6, 7)
HEADS = 8
HD = 64
VD = 128
EXPERTS = 16
GROUPS = 4
PER_GROUP = EXPERTS // GROUPS
SLOTS = P
STEPS = GROUPS + 1
STEP_BLOCKS = 3 * PER_GROUP
ALPHA = (2.0 * LAYERS) ** 0.25
LN_EPS = 1e-5
RMS_EPS = 1e-6
LAMBDA_INIT = 0.8 - 0.6 * math.exp(-0.3 * 1)
MASKED = -1e30
TAKEN = -3e38
TOPK = min(256, T // 4)
IDX_HEADS = 4
HH = 4
CHUNK = 64
CW = 512
LEVELS = (2, 4, 8, 16, 32, 64, 128)
BIAS_LINE = 512
BETWEEN = {0: ("hg",), 1: ("gates", 0), 2: ("gates", 1), 3: ("gates", 2), 4: ("gates", 3), 5: ("gates", 4),
           6: ("gates", 5)}

C_AQ, C_AK, C_IQ, C_IK, C_HQ, C_HF, C_HI, C_HG, C_CB, C_CC, C_CH, C_GATES = (
    0, 512, 768, 1024, 1092, 1604, 2116, 2628, 3140, 3652, 4164, 4676)
IKW = C_HQ - C_IK

R_CLG, R_CLB, R_BDW, R_MIXG, R_MIXB, R_FFNG, R_FFNB, R_MIX2, R_MLP2, R_CW2 = (
    0, 8, 16, 24, 40, 56, 72, 88, 96, 104)
R_ROWS = 116


def program(nc, a, out):
    ctx = ExitStack()
    with ctx:
        def sb(name, shape, dt=F32):
            return ctx.enter_context(nc.sbuf_tensor(name, shape, dt))

        sems = {}

        def sem(name):
            if name not in sems:
                sems[name] = ctx.enter_context(nc.semaphore(name))
            return sems[name]

        ring = sb("ring", [P, RING, BLK])
        xtok = sb("xtok", [P, NT, D])
        xT = sb("xT", [P, KD, T])
        res = sb("res", [P, NT, D])
        rows = [sb(f"rows{i}", [P, 2, D]) for i in range(2)]
        ident = sb("ident", [P, P])
        ones = sb("ones", [P, P])
        mean_w = sb("mean_w", [P, P])
        earlier = sb("earlier", [P, P])
        iota = sb("iota", [P, STEPS * SLOTS])
        lower_e = sb("lower_e", [P, PER_GROUP, PER_GROUP])
        first_g = sb("first_g", [P, GROUPS])
        index_g = sb("index_g", [P, GROUPS])
        params = sb("params", [P, P])
        pcol = sb("pcol", [P, R_ROWS])
        wdw = sb("wdw", [P, CONV * KD])
        rw = sb("rw", [P, KD, EXPERTS])
        rbias = sb("rbias", [P, EXPERTS])
        eps_ln = sb("eps_ln", [P, 1])
        eps_rms = sb("eps_rms", [P, 1])
        lamb = sb("lamb", [P, 4, HD])
        lam = sb("lam", [P, 8])
        subg = sb("subg", [P, VD])
        qg = sb("qg", [P, HD])
        kg = sb("kg", [P, HD])
        hng = sb("hng", [P, VD])
        tables = sb("tables", [33, 2 * HEADS])
        stats = sb("stats", [P, NT, 2, 6])
        mv = sb("mv", [P, NT, 2])
        rstd = sb("rstd", [P, NT, 2])
        small = sb("small", [P, 900])
        ARENA = 20120
        arena = sb("arena", [P, ARENA])

        def carve(start):
            at = [start]

            def take(*shape):
                n = math.prod(shape)
                view = arena[:, at[0]:at[0] + n]
                at[0] += n
                assert at[0] <= ARENA, at[0]
                names = "abc"[:len(shape)]
                if len(shape) > 1:
                    view = view.rearrange(f"p ({' '.join(names)}) -> p {' '.join(names)}",
                                          **dict(zip(names, shape)))
                return view
            take.at = at
            return take

        take = carve(0)
        glu = take(NT, D)
        gate_in = take(2, HALF)
        b1row = take(2 * D)
        diag = take(len(PE_CHUNKS), P)
        b2row = take(D)
        hpad = take(KD, CONV - 1 + T)
        conv = take(KD, T)
        squares = take(KD, T)
        cstd = take(2, T)
        wst = take(2, P)
        onehot = take(BIAS_LINE)
        line = take(BIAS_LINE)
        shifted = take(2, HEADS * T)
        reverse = take(P)
        take = carve(0)
        sel_slots = take(NT, STEPS * SLOTS)
        slots_T = take(STEPS, T)
        xg_all = take(KD, STEPS * SLOTS)
        xg = take(KD, SLOTS)
        sg = take(2, HALF)
        hx = take(2, HALF)
        hxT = take(2, 4, P)
        y_sb = take(STEPS, D)
        take = carve(0)
        kT = take(KD, T)
        qT = take(KD, T)
        vtok = take(NT, D)
        bias1 = take(HEADS, T)
        logit = take(2, 2, T)
        prob = take(2, 2, T)
        diffp = take(2, T)
        diffT = take(2, 2, P)
        otok = take(NT, D)
        osq = take(D)
        take = carve(0)
        akv = take(NT, HALF)
        qaT = take(4, T)
        bias2 = take(HEADS, T)
        mb0 = take(HEADS, P)
        mb = [mb0, bias2]
        s2 = take(2, 2, T)
        pT2 = take(2, 2, P)
        assert take.at[0] >= 6 * NT * HALF
        aq = take(NT, HALF)
        asq = take(HALF)
        kd = take(NT, 2, 2 * HD)
        ikd = take(NT, 2 * HD)
        iqT = take(2, T)
        ikT = take(T)
        ikw = take(NT, IKW)
        kaT = take(2, T)
        iscore = take(NT, T)
        qh = take(HH, T)
        zf = take(HH, T)
        kk = take(HH, T)
        gcum = take(HH, T)
        ez = take(HH, T)
        ke = take(HH, T)
        itok = take(NT, CW)
        yaT = take(4, T)
        upad = take(4, 2 + T)
        reset = ke
        qe = zf

        def again(first, *shape):
            return carve(first)(*shape)
        A_AQ = 6656
        relus = again(A_AQ, IDX_HEADS, T)
        yat = again(A_AQ, NT, CW)
        yhT = again(A_AQ, 4, T)
        att01 = again(A_AQ + 1024, HH, P)
        masked = again(A_AQ + 1536, HH, P)
        attT = again(A_AQ + 2048, NT, HH, P)
        gates = again(0, 6, NT, HALF)
        cc = rows[0][:, 0, :].rearrange("p (c t) -> p c t", c=4)
        ch = rows[0][:, 1, :].rearrange("p (c t) -> p c t", c=4)
        cb = rows[1][:, 0, :].rearrange("p (c t) -> p c t", c=4)
        ycT = rows[1][:, 1, :].rearrange("p (c t) -> p c t", c=4)
        yh = res[:, 0, :].rearrange("p (t n) -> p t n", t=NT)
        hgs = res[:, 1, :].rearrange("p (t n) -> p t n", t=NT)
        blockmask = sb("blockmask", [P, len(LEVELS), P])
        mixed = res
        take = carve(0)
        mr = take(2, NT, HALF)
        mh = take(2, NT, HALF)
        mhT = take(2, 4, T)

        at = [0]

        def tiny(*shape):
            n = math.prod(shape)
            v = small[:, at[0]:at[0] + n]
            at[0] += n
            assert at[0] <= small.shape[1], at[0]
            if len(shape) > 1:
                names = "abcd"[:len(shape)]
                v = v.rearrange(f"p ({' '.join(names)}) -> p {' '.join(names)}", **dict(zip(names, shape)))
            return v
        NG = NT * GROUPS
        aff = tiny(NT, EXPERTS)
        sel = tiny(NG, PER_GROUP)
        pair_hi = tiny(NG, 2)
        pair_lo = tiny(NG, 2)
        top = tiny(3, NG)
        gscore = tiny(NT, GROUPS)
        gbest = tiny(NT)
        gkey = tiny(NT, GROUPS)
        in_group = tiny(NT, GROUPS)
        beats = tiny(NG, PER_GROUP, PER_GROUP)
        ties = tiny(NG, PER_GROUP, PER_GROUP)
        place = tiny(NG, PER_GROUP)
        gsum = tiny(NT)
        gates4 = tiny(NT, PER_GROUP)
        pos = tiny(NT, GROUPS)
        slot = tiny(3, NT)
        over = tiny(2, GROUPS)
        slot_gates = tiny(STEPS * PER_GROUP)
        dmax_n = tiny(2, 2)
        dneg = dmax_n
        dsum = tiny(2, 2)
        dinv = tiny(2, 2)
        oms = tiny(NT, HEADS)
        ostd = tiny(NT, HEADS)
        qkms = tiny(NT, 10)
        qkstd = tiny(NT, 10)
        aneg = tiny(2, 2)
        asum = tiny(NT, HEADS)
        ainv = tiny(NT, HEADS)
        top8 = tiny(8)
        iws = tiny(NT, IDX_HEADS)
        hms = tiny(NT, HH)
        hstd = tiny(NT, HH)
        one1 = tiny(1)
        over_group = [sb(f"over_group{l}", [1, 2], I32) for l in range(LAYERS)]

        lines = nc.dram_tensor("bias_lines", (2 * HEADS, BIAS_LINE), F32, kind="Internal")
        biases = nc.dram_tensor("biases", (P, 2, HEADS * T), F32, kind="Internal")
        banks = [ctx.enter_context(nc.psum_tensor(f"bank{i}", [P, HALF], F32)) for i in range(8)]

        bank_ready = [sem(f"bank{i}_ready") for i in range(8)]
        bank_free = [sem(f"bank{i}_free") for i in range(8)]
        uses, count = {}, [0] * 8

        def use(label, b):
            uses[label] = (b, count[b], 0)
            count[b] += 1

        def use_loop(labels, times):
            per = [0] * 8
            for label, b in labels:
                per[b] += 1
            seen = [0] * 8
            for label, b in labels:
                uses[label] = (b, count[b] + seen[b], per[b])
                seen[b] += 1
            for b in range(8):
                count[b] += per[b] * times

        def nth(label, i):
            b, n, per = uses[label]
            return n + per * i if per else n

        def bank(label):
            return banks[uses[label][0]]

        def claim(pe, label, i=0):
            if uses[label][1] or uses[label][2]:
                pe.wait_ge(bank_free[uses[label][0]], nth(label, i))

        def ready(eng, label, i=0):
            eng.wait_ge(bank_ready[uses[label][0]], nth(label, i) + 1)

        def freed(eng, label, i=0):
            eng.wait_ge(bank_free[uses[label][0]], nth(label, i) + 1)

        def full(ins, label):
            ins.then_inc(bank_ready[uses[label][0]], 1)

        def free(ins, label):
            ins.then_inc(bank_free[uses[label][0]], 1)

        def use_transposes(name):
            for b in range(4):
                use((name, b), 4 + b)

        def use_moe(l):
            use(("router", l), 4)
            use(("rank", l), 5)
            for c in range(KD):
                use(("gather", l, c), c % 4)
            for b in range(2):
                use(("gather_over", l, b), b)
            for b in range(3):
                use(("slotsT", l, b), 4 + b)
            use(("slot_gates", l), 7)
            loop = []
            for e in range(PER_GROUP):
                loop += [(("gate", l, e), e % 2 * 2), (("up", l, e), e % 2 * 2 + 1), (("hT", l, e), 4 + e % 2)]
            loop += [(("y", l, 0), 6), (("y", l, 1), 7)]
            use_loop(loop, STEPS)
            for t in range(NT):
                for h in range(2):
                    use(("scatter", l, t, h), 2 * t + h)

        lin = [0]

        def use_lin(label):
            use(label, lin[0] % 4)
            lin[0] += 1

        use_transposes("x")
        for half in range(2):
            for kind in ("a", "g"):
                for t in range(NT):
                    use_lin(("pw1", kind, half, t))
            if half == 0:
                use("params", 6)
                use("taps", 7)
                use("line", 5)
            for b in range(2):
                use(("glu", half, b), 4 + b)
        for n, c in enumerate(PE_CHUNKS):
            use(("tap", c), 4 + n)
        use("conv_mean", 6)
        use("conv_var", 7)
        for table in range(2):
            for q in range(4):
                use(("bias", table, q), 4 + q)
        for half in range(2):
            for t in range(NT):
                use_lin(("pw2", half, t))
        use_transposes("ln0")
        use_moe(0)
        use_transposes("ln1")
        for n in range(KD):
            use_lin(("k", n))
        for n in range(KD):
            use_lin(("q", n))
        for half in range(2):
            for t in range(NT):
                use_lin(("v", half, t))
        units = [(qt, h) for qt in range(NT) for h in range(HEADS)]
        for u, (qt, h) in enumerate(units):
            use_lin(("s", u))
            use(("pT", u), 4 + u % 2)
            if h % 4 == 0:
                use(("o", qt, h // 4), 6 + h // 4)
        use_transposes("o")
        for half in range(2):
            for t in range(NT):
                use_lin(("wo", half, t))
        use_transposes("ln2")
        use_moe(1)
        use_transposes("rm0")
        for name in ("ikw", "akv", "aq"):
            for t in range(NT):
                use_lin((name, t))
        for b in range(2):
            use(("qaT", b), 4 + b)
        use("kaT", 6)
        use("iqT", 7)
        use("ikT", 4)
        for name in ("hf", "hq"):
            for n in range(4):
                use_lin((name, n))
        for t in range(NT):
            use_lin(("hi", t))
        for qt in range(NT):
            for b in range(2):
                use(("is", qt, b), 5 + b)
        for name in ("cc", "ch", "cb"):
            for n in range(4):
                use_lin((name, n))
        for qt in range(NT):
            for u in range(4):
                use_lin(("s2", qt, u))
                for j in range(2):
                    use(("p2T", qt, u, j), 4 + j)
            use(("o2", qt), 6 + qt)
        for b in range(2):
            use(("yaT", b), 4 + b)
        for n in range(len(LEVELS) + 1):
            for t in range(NT):
                use_lin(("lev", n, t))
            if n in BETWEEN:
                for t in range(NT):
                    use_lin((*BETWEEN[n], t))
        use_lin("lev01")
        for t in range(NT):
            use_lin(("oh", t))
        for b in range(2):
            use(("yhT", b), 4 + b)
        for br in range(3):
            for t in range(NT):
                for h in range(2):
                    use_lin(("branch", br, t, h))
        use_transposes("mixed")
        for h in range(2):
            for t in range(NT):
                use_lin(("out", h, t))
        use_transposes("rm1")
        loop = []
        for j in range(2):
            loop += [(("mu", j, t), t) for t in range(NT)] + [(("mT", j, t), 2 + t) for t in range(NT)]
        use_loop(loop, 4)
        for t in range(NT):
            for h in range(2):
                use(("md", t, h), 4 + 2 * t + h)

        slot_landed = [sem(f"slot{i}_landed") for i in range(RING)]
        blocks, order = {}, []

        def add(label, src, cols, read, per=0):
            n = len(order)
            blocks[label] = dict(n=n, slot=n % RING, turn=n // RING, src=src, cols=cols, read=read, per=per)
            order.append(label)

        def wide(w, c0, n):
            return w[:, c0:c0 + n].rearrange("(k p) n -> p k n", p=P)

        def deep(w):
            return w.rearrange("(k p) n -> p k n", p=P)

        w1 = a["a_w_pw1"][0]
        for half in range(2):
            for k, kind in enumerate(("a", "g")):
                add(("pw1", kind, half), wide(w1, k * D + half * HALF, HALF), HALF, ("pw1", kind, half, NT - 1))
        for half in range(2):
            add(("pw2", half), wide(a["a_w_pw2"][0], half * HALF, HALF), HALF, ("pw2", half, NT - 1))

        MOE_ORDER = [("gate", 0), ("up", 0)]
        for e in range(1, PER_GROUP):
            MOE_ORDER += [("gate", e), ("up", e), ("down", e - 1)]
        MOE_ORDER += [("down", PER_GROUP - 1)]
        assert len(MOE_ORDER) == STEP_BLOCKS and STEP_BLOCKS % RING == 0

        def add_moe(l):
            per = STEP_BLOCKS // RING
            for kind, e in MOE_ORDER:
                if kind == "down":
                    read = ("y", l, 1) if e == PER_GROUP - 1 else ("down_read", l, e)
                else:
                    read = (kind, l, e)
                add((kind, l, e), None, D if kind == "down" else HALF, read, per)
            order.extend([None] * (STEP_BLOCKS * (STEPS - 1)))

        add_moe(0)
        wkv, wq = a["w_kv"], a["b_w_q"][0]
        for half in range(2):
            add(("k", half), wide(wkv, half * HALF, HALF), HALF, ("k", 4 * half + 3))
        for half in range(2):
            add(("q", half), wide(wq, half * HALF, HALF), HALF, ("q", 4 * half + 3))
        for half in range(2):
            add(("v", half), wide(wkv, D + half * HALF, HALF), HALF, ("v", half, NT - 1))
        for half in range(2):
            add(("wo", half), wide(a["b_w_o"][0], half * HALF, HALF), HALF, ("wo", half, NT - 1))
        add_moe(1)
        win = a["w_in_2"][0]
        add("ikw", wide(win, C_IK, IKW), IKW, ("ikw", NT - 1))
        add("akv", wide(win, C_AK, HALF), HALF, ("akv", NT - 1))
        add("aq", wide(win, C_AQ, HALF), HALF, ("aq", NT - 1))
        add("hf", wide(win, C_HF, HALF), HALF, ("hf", 3))
        add("hq", wide(win, C_HQ, HALF), HALF, ("hq", 3))
        add("hi", wide(win, C_HI, HALF), HALF, ("hi", NT - 1))
        for name, c0 in (("cc", C_CC), ("ch", C_CH), ("cb", C_CB)):
            add(name, wide(win, c0, HALF), HALF, (name, 3))
        add("hg", wide(win, C_HG, HALF), HALF, ("hg", NT - 1))
        for j in range(6):
            add(("gates", j), wide(win, C_GATES + j * HALF, HALF), HALF, ("gates", j, NT - 1))
        for br, name in enumerate(("w_up_attn_2", "w_up_hgrn_2", "w_up_conv_2")):
            add(("branch", br), deep(a[name][0]), D, ("branch", br, NT - 1, 1))
        for h in range(2):
            add(("out", h), wide(a["w_out_2"][0], h * HALF, HALF), HALF, ("out", h, NT - 1))
        MLP_ORDER = [("mu", 0), ("mu", 1), ("md", 0), ("md", 1)]
        assert len(MLP_ORDER) == RING
        for kind, j in MLP_ORDER:
            add((kind, j), None, HALF if kind == "mu" else D, ("mu", j, NT - 1) if kind == "mu" else "md_read", 1)
        order.extend([None] * 12)

        def block(label):
            b = blocks[label]
            w = ring[:, b["slot"], 0:BLK if b["cols"] != IKW else KD * IKW]
            return w.rearrange("p (k n) -> p k n", n=b["cols"])

        def landed(pe, label, i=0):
            b = blocks[label]
            pe.wait_ge(slot_landed[b["slot"]], 16 * (b["turn"] + 1) + 16 * b["per"] * i)

        def was_read(eng, label, i=0):
            r = blocks[label]["read"]
            if r == "md_read":
                eng.wait_ge(sem("md_read"), 2 * i + label[1] + 1)
            elif r[0] == "down_read":
                eng.wait_ge(sem(f"down_read{r[1]}"), (PER_GROUP - 1) * i + r[2] + 1)
            else:
                ready(eng, r, i)

        def spilled(eng, l):
            eng.wait_ge(sem(f"over_known{l}"), 1)
            return eng.value_load(over_group[l][0:1, 0:1], min_val=0, max_val=1)

        def skipped(eng, sems_, labels):
            for label in labels:
                last = (ready if sems_ is bank_ready else freed)
                last(eng, label, GROUPS - 1)
                eng.sem_inc(sems_[uses[label][0]], uses[label][2])

        blk = ctx.enter_context(nc.Block())

        def unit_heads(u):
            return 4 * (u // 2) + u % 2, 4 * (u // 2) + u % 2 + 2

        @blk.sync
        def _(sp):
            sp.dma_start(xtok[:], a["x"][0].rearrange("(t p) d -> p t d", p=P)).then_inc(sem("x_in"), 16)

            def load(label, src=None):
                b = blocks[label]
                sp.dma_start(block(label), b["src"] if src is None else src)\
                  .then_inc(slot_landed[b["slot"]], 16)

            def stream(first, last):
                for n in range(first, last):
                    if n >= RING:
                        before = order[n - RING]
                        if before is not None:
                            was_read(sp, before)
                        else:
                            where, i = loop_end[n - RING]
                            was_read(sp, where, i)
                    if blocks[order[n]]["src"] is not None:
                        load(order[n])

            loop_end = {}
            for l in range(LAYERS):
                n0 = blocks[("gate", l, 0)]["n"]
                for j in range(STEP_BLOCKS):
                    kind, e = MOE_ORDER[j]
                    loop_end[n0 + (STEPS - 1) * STEP_BLOCKS + j] = ((kind, l, e), STEPS - 1)

            def load_expert(l, j, group):
                kind, e = MOE_ORDER[j]
                w = a[f"moe_w_{kind}"][l].rearrange("e (k p) n -> p e k n", p=P)
                load((kind, l, e), w[:, bass.ds(group * PER_GROUP + e, 1), :, :].rearrange("p e k n -> p (e k) n"))

            def experts(l):
                n0 = blocks[("gate", l, 0)]["n"]
                for j in range(RING):
                    was_read(sp, order[n0 + j - RING])
                    load_expert(l, j, 0)

                def rest(i, group, following):
                    for j in range(RING, STEP_BLOCKS):
                        kind, e = MOE_ORDER[j - RING]
                        was_read(sp, (kind, l, e), i)
                        load_expert(l, j, group)
                    if following is None:
                        return
                    for j in range(RING):
                        kind, e = MOE_ORDER[j + STEP_BLOCKS - RING]
                        was_read(sp, (kind, l, e), i)
                        load_expert(l, j, following)

                with sp.Fori(0, GROUPS - 1) as i:
                    rest(i, i, i + 1)
                sp.wait_ge(sem(f"over_known{l}"), 1)
                more = spilled(sp, l)
                over = sp.value_load(over_group[l][0:1, 1:2], min_val=0, max_val=GROUPS - 1)
                rest(GROUPS - 1, GROUPS - 1, None)
                with sp.If(more > 0):
                    for j in range(RING):
                        kind, e = MOE_ORDER[j + STEP_BLOCKS - RING]
                        was_read(sp, (kind, l, e), GROUPS - 1)
                        load_expert(l, j, over)
                    rest(GROUPS, over, None)
                with sp.Else():
                    for kind, e in MOE_ORDER[-RING:]:
                        landed(sp, (kind, l, e), GROUPS - 1)
                        sp.sem_inc(slot_landed[blocks[(kind, l, e)]["slot"]], 16 * STEP_BLOCKS // RING)

            moe_n = [blocks[("gate", l, 0)]["n"] for l in range(LAYERS)]
            mlp_n = blocks[("mu", 0)]["n"]
            stream(0, moe_n[0])
            experts(0)
            stream(moe_n[0] + STEPS * STEP_BLOCKS, moe_n[1])
            experts(1)
            stream(moe_n[1] + STEPS * STEP_BLOCKS, mlp_n)
            wmu = a["w_mlp_up_2"][0].rearrange("(k p) (j n) -> p k j n", p=P, n=HALF)
            wmd = a["w_mlp_down_2"][0].rearrange("(j k p) n -> p j k n", p=P, k=4)

            def load_mlp(m, i):
                kind, j = MLP_ORDER[m]
                if kind == "mu":
                    src = wmu[:, :, bass.ds(i * 2 + j, 1), :].rearrange("p k j n -> p k (j n)")
                else:
                    src = wmd[:, bass.ds(i * 2 + j, 1), :, :].rearrange("p j k n -> p (j k) n")
                load((kind, j), src)
            for m in range(RING):
                was_read(sp, order[mlp_n + m - RING])
                load_mlp(m, 0)
            with sp.Fori(0, 3) as i:
                for m in range(RING):
                    was_read(sp, MLP_ORDER[m], i)
                    load_mlp(m, i + 1)
            for t in range(NT):
                sp.wait_ge(sem("result"), t + 1)
                sp.dma_start(out[0, t * P:(t + 1) * P, :], res[:, t, :]).then_inc(sem("stored"), 16)
            sp.wait_ge(sem("stored"), 16 * NT)

        @blk.gpsimd
        def _(pool):
            g = nc.gpsimd
            g.memset(ident[:], 0.0).then_inc(sem("c0"), 1)
            g.memset(ones[:], 1.0).then_inc(sem("c0"), 1)
            g.memset(mean_w[:], 1.0 / D).then_inc(sem("consts"), 1)
            g.memset(eps_ln[:], LN_EPS).then_inc(sem("consts"), 1)
            g.memset(one1, 1.0).then_inc(sem("consts"), 1)
            g.memset(eps_rms[:], RMS_EPS).then_inc(sem("consts"), 1)
            pool.wait_ge(sem("c0"), 2)
            g.affine_select(out=ident[:], in_=ident[:], compare_op=ALU.not_equal, fill=1.0, base=0,
                            pattern=[[-1, P]], channel_multiplier=1).then_inc(sem("ident"), 1)
            g.memset(reverse, 0.0).then_inc(sem("reverse"), 1)
            pool.wait_ge(sem("reverse"), 1)
            g.affine_select(out=reverse, in_=reverse, compare_op=ALU.not_equal, fill=1.0, base=1 - P,
                            pattern=[[1, P]], channel_multiplier=1).then_inc(sem("reverse"), 1)
            g.memset(hpad[:, :, 0:CONV - 1], 0.0).then_inc(sem("hpad0"), 1)
            g.affine_select(out=earlier[:], in_=ones[:], compare_op=ALU.is_gt, fill=0.0, base=0,
                            pattern=[[1, P]], channel_multiplier=-1).then_inc(sem("consts"), 1)
            g.affine_select(out=lower_e[:], in_=ones[:, 0:16].rearrange("p (a b) -> p a b", a=4),
                            compare_op=ALU.is_gt, fill=0.0, base=0,
                            pattern=[[1, 4], [-1, 4]], channel_multiplier=0).then_inc(sem("consts"), 1)
            g.iota(iota[:], pattern=[[1, STEPS * SLOTS]], base=0, channel_multiplier=0,
                   allow_small_or_imprecise_dtypes=True).then_inc(sem("consts"), 1)
            g.iota(index_g[:], pattern=[[1, GROUPS]], base=0, channel_multiplier=0,
                   allow_small_or_imprecise_dtypes=True).then_inc(sem("consts"), 1)
            g.iota(first_g[:], pattern=[[-1, GROUPS]], base=GROUPS, channel_multiplier=0,
                   allow_small_or_imprecise_dtypes=True).then_inc(sem("consts"), 1)
            for n, b in enumerate(LEVELS):
                m = blockmask[:, n, :].rearrange("p (c b) -> p c b", b=b)
                src = ones[:].rearrange("p (c b) -> p c b", b=b)
                g.affine_select(out=m, in_=src, compare_op=ALU.is_ge, fill=0.0, base=0,
                                pattern=[[-b, P // b], [0, b]], channel_multiplier=1).then_inc(sem("mask"), 1)
                pool.wait_ge(sem("mask"), 3 * n + 1)
                g.affine_select(out=m, in_=m, compare_op=ALU.is_gt, fill=0.0, base=b // 2,
                                pattern=[[b, P // b], [0, b]], channel_multiplier=-1).then_inc(sem("mask"), 1)
                pool.wait_ge(sem("mask"), 3 * n + 2)
                g.affine_select(out=m, in_=m, compare_op=ALU.is_ge, fill=0.0, base=-(b // 2),
                                pattern=[[0, P // b], [1, b]], channel_multiplier=0).then_inc(sem("mask"), 1)

            def tok(n):
                r = rows[n % 2]
                pool.wait_ge(sem(f"rows{n}"), 32)
                pool.wait_ge(sem(f"ln{n}_xhat"), NT)
                gr = r[:, 0:1, :].broadcast_to([P, NT, D])
                br = r[:, 1:2, :].broadcast_to([P, NT, D])
                g.tensor_tensor(xtok[:], res[:], gr, ALU.mult).then_inc(sem(f"ln{n}_tok"), 1)
                pool.wait_ge(sem(f"ln{n}_tok"), 1)
                g.tensor_tensor(xtok[:], xtok[:], br, ALU.add).then_inc(sem(f"ln{n}_tok"), 1)
                if n + 2 < 2 * LAYERS:
                    pool.wait_ge(sem(f"ln{n}_tok"), 2)
                    load_rows(n + 2)

            def load_rows(n):
                l = n // 2
                gsrc, bsrc = (a["ln_mix_g"], a["ln_mix_b"]) if n % 2 == 0 else (a["ln_ffn_g"], a["ln_ffn_b"])
                for k, src in enumerate((gsrc, bsrc)):
                    pool.dma_start(rows[n % 2][:, k, :], src[l:l + 1, :].broadcast_to([P, D]))\
                        .then_inc(sem(f"rows{n}"), 16)

            def experts(l):
                def copy(i):
                    g.tensor_copy(xg[:], xg_all[:, :, bass.ds(i * SLOTS, SLOTS)]).then_inc(sem(f"xg{l}"), 1)
                for c in range(4, KD):
                    freed(pool, ("gather", l, c))
                for b in range(2):
                    freed(pool, ("gather_over", l, b))
                copy(0)
                def next_copy(i):
                    ready(pool, ("up", l, PER_GROUP - 1), i - 1)
                    copy(i)
                more = spilled(pool, l)
                with pool.Fori(1, GROUPS) as i:
                    next_copy(i)
                with pool.If(more > 0):
                    next_copy(GROUPS)
                with pool.Else():
                    pool.wait_ge(sem(f"xg{l}"), GROUPS)
                    pool.sem_inc(sem(f"xg{l}"), 1)

            for half in range(2):
                for t in range(NT):
                    freed(pool, ("pw1", "a", half, t))
                    freed(pool, ("pw1", "g", half, t))
                    x = glu[:, t, half * HALF:(half + 1) * HALF]
                    g.tensor_tensor(x, x, gate_in[:, t, :], ALU.mult).then_inc(sem("glu"), 1)
            load_rows(0)
            load_rows(1)
            pool.wait_ge(sem("lines"), 16)
            for table in range(2):
                pool.dma_start(shifted[:, table, :].rearrange("p (h k) -> p h k", h=HEADS),
                               bass.AP(lines, table * HEADS * BIAS_LINE, [[1, P], [BIAS_LINE, HEADS], [1, T]]))\
                    .then_inc(sem("shifted"), 16)
            tok(0)
            experts(0)
            tok(1)
            pool.wait_ge(sem("biases"), 16)
            for t in range(NT):
                for h in range(2):
                    freed(pool, ("scatter", 0, t, h))
            pool.dma_start(bias1.rearrange("p h k -> p (h k)"), biases.ap()[:, 0, :]).then_inc(sem("bias1"), 16)
            tok(2)
            experts(1)
            for t in range(NT):
                for h in range(2):
                    freed(pool, ("scatter", 1, t, h))
            pool.dma_start(bias2.rearrange("p h k -> p (h k)"), biases.ap()[:, 1, :]).then_inc(sem("bias2"), 16)
            r4 = reset.rearrange("p h (c t) -> p (h c) t", t=CHUNK)
            g.memset(r4, 1.0).then_inc(sem("reset"), 1)
            pool.wait_ge(sem("reset"), 1)
            g.memset(r4[:, :, 0:1], 0.0).then_inc(sem("reset"), 1)
            g.memset(upad[:, :, 0:2], 0.0).then_inc(sem("upad0"), 1)
            for qt in range(NT):
                n = (qt + 1) * P
                pool.wait_ge(sem("isc"), qt + 1)
                v = iscore[:, qt, 0:n]
                g.affine_select(out=v, in_=v, compare_op=ALU.is_ge, fill=MASKED, base=qt * P,
                                pattern=[[-1, n]], channel_multiplier=1).then_inc(sem("causal"), 1)
            for qt in range(NT):
                n = (qt + 1) * P
                if qt == 0:
                    pool.wait_ge(sem("bias2"), 16)
                else:
                    pool.wait_ge(sem("mb"), qt)
                pool.wait_ge(sem("chosen"), qt + 1)
                am = iscore[:, qt:qt + 1, 0:n].broadcast_to([P, HEADS, n])
                g.tensor_tensor(mb[qt], bias2[:, :, P - qt * P:T], am, ALU.add).then_inc(sem("mb"), 1)

        @blk.scalar
        def _(act):
            s = nc.scalar
            def par(dst, src, name):
                act.dma_start(dst, src).then_inc(sem(name), 16)

            def chunks(v):
                return v.rearrange("l (c p) -> (l c) p", p=P)
            par(b1row[0:1, :], a["a_b_pw1"], "par_b1")
            for r0, src in ((R_CLG, a["a_ln_g"]), (R_CLB, a["a_ln_b"]), (R_BDW, a["a_b_dw"]),
                            (R_MIXG, a["ln_mix_g"]), (R_MIXB, a["ln_mix_b"]), (R_FFNG, a["ln_ffn_g"]),
                            (R_FFNB, a["ln_ffn_b"]), (R_MIX2, a["ln_mix_g_2"]), (R_MLP2, a["ln_mlp_g_2"]),
                            (R_CW2, a["conv_w_2"][0])):
                src = chunks(src)
                par(params[r0:r0 + src.shape[0], :], src, "par_rows")
            taps = a["a_w_dw"][0].rearrange("j (c p) -> (j c) p", p=P)
            for n in range(2):
                par(wst[0:124, n, :], taps[n * 124:(n + 1) * 124, :], "par_taps")
            par(b2row, a["a_b_pw2"].broadcast_to([P, D]), "par_b2")
            par(rw[:], a["router_w"].rearrange("(k p) e -> p k e", p=P), "par_router")
            par(rbias[:], a["router_bias"].rearrange("(o e) -> o e", o=1).broadcast_to([P, EXPERTS]), "par_router")
            par(tables[0:32, 0:HEADS], a["rel_bias"], "par_tables")
            par(tables[0:32, HEADS:], a["rel_bias_2"], "par_tables")
            par(onehot[0:33, :], a["bucket_onehot"], "par_tables")
            par(lamb[:].rearrange("p a b -> p (a b)"),
                a["b_lambda"].rearrange("o a b -> o (a b)").broadcast_to([P, 4 * HD]), "par_gains")
            par(subg[:], a["b_subln_g"].broadcast_to([P, VD]), "par_gains")
            par(qg[:], a["q_norm_g_2"].broadcast_to([P, HD]), "par_gains")
            par(kg[:], a["k_norm_g_2"].broadcast_to([P, HD]), "par_gains")
            par(hng[:], a["hgrn_norm_g_2"].broadcast_to([P, VD]), "par_gains")

            def copy(dst, src):
                return s.activation(dst, src, ACT.Copy)

            def evac_T(name, dst, gain=None, shift=None):
                for b in (0, 2):
                    ready(act, (name, b))
                    for c in (2 * b, 2 * b + 1):
                        src = bank((name, b))[:, c % 2 * T:c % 2 * T + T]
                        if gain is None:
                            last = copy(dst[:, c, :], src)
                        elif shift is None:
                            last = s.activation(dst[:, c, :], src, ACT.Copy, scale=pcol[:, gain + c:gain + c + 1])
                        else:
                            last = s.activation(dst[:, c, :], src, ACT.Identity,
                                                scale=pcol[:, gain + c:gain + c + 1],
                                                bias=pcol[:, shift + c:shift + c + 1])
                    free(last, (name, b))

            def std(n, eps):
                for t in range(NT):
                    act.wait_ge(sem(f"{n}_var"), t + 1)
                    s.activation(rstd[:, t, 0:1], mv[:, t, 1:2], ACT.Sqrt, bias=eps[:]).then_inc(sem(f"{n}_std"), 1)

            evac_T("x", xT)
            for half in range(2):
                for t in range(NT):
                    ready(act, ("pw1", "a", half, t))
                    free(copy(glu[:, t, half * HALF:(half + 1) * HALF], bank(("pw1", "a", half, t))[:]),
                         ("pw1", "a", half, t))
                for t in range(NT):
                    ready(act, ("pw1", "g", half, t))
                    if half:
                        act.wait_ge(sem("glu"), NT)
                    free(s.activation(gate_in[:, t, :], bank(("pw1", "g", half, t))[:], ACT.Sigmoid),
                         ("pw1", "g", half, t))
                if half == 0:
                    ready(act, "params")
                    free(copy(pcol[:], bank("params")[:, 0:R_ROWS]), "params")
                    ready(act, "taps")
                    free(copy(wdw[:], bank("taps")[:, 0:CONV * KD]), "taps")
                    ready(act, "line")
                    free(copy(line[0:2 * HEADS, :], bank("line")[0:2 * HEADS, :]), "line")
                    freed(act, "line")
                    act.dma_start(lines.ap(), line[0:2 * HEADS, :]).then_inc(sem("lines"), 16)
                    act.wait_ge(sem("hpad0"), 1)
                for b in range(1 + half):
                    ready(act, ("glu", half, b))
                    for j in range(2):
                        last = copy(hpad[:, 4 * half + 2 * b + j, CONV - 1:], bank(("glu", half, b))[:, j * T:(j + 1) * T])
                    free(last, ("glu", half, b))

            def diagonals(j, first=False):
                for n, c in enumerate(PE_CHUNKS):
                    if not first:
                        act.wait_ge(sem(f"diag{n}_read"), j)
                    s.activation(diag[:, n, :], ident[:], ACT.Copy, scale=wdw[:, bass.ds(j * KD + c, 1)])\
                     .then_inc(sem(f"diag{n}"), 1)
            freed(act, "taps")
            freed(act, "params")
            act.wait_ge(sem("ident"), 1)
            diagonals(0, first=True)
            with act.Fori(1, CONV) as j:
                diagonals(j)
            for c in PE_CHUNKS:
                ready(act, ("tap", c))
                free(s.activation(conv[:, c, :], bank(("tap", c))[:, 0:T], ACT.Identity,
                                  bias=pcol[:, R_BDW + c:R_BDW + c + 1]), ("tap", c))
            freed(act, "conv_mean")
            s.activation(squares, conv, ACT.Square).then_inc(sem("conv_sq"), 1)
            ready(act, "conv_var")
            free(s.activation(cstd[:, 0, :], bank("conv_var")[:, 0:T], ACT.Sqrt, bias=eps_ln[:]), "conv_var")
            act.wait_ge(sem("conv_normal"), 1)
            for c in range(KD):
                s.activation(xT[:, c, :], conv[:, c, :], ACT.Silu, scale=pcol[:, R_CLG + c:R_CLG + c + 1],
                             bias=pcol[:, R_CLB + c:R_CLB + c + 1]).then_inc(sem("conv_silu"), 1)

            for q in range(4):
                freed(act, ("bias", 1, q))
            act.dma_start(biases.ap(), shifted).then_inc(sem("biases"), 16)

            def experts(l):
                ready(act, ("router", l))
                free(s.activation(aff, bank(("router", l))[:, 0:NT * EXPERTS], ACT.Sigmoid), ("router", l))
                for c in range(0, KD, 2):
                    ready(act, ("gather", l, c))
                    free(copy(xg_all[:, c, 0:HALF], bank(("gather", l, c))[:]), ("gather", l, c))
                ready(act, ("gather_over", l, 0))
                free(copy(xg_all[:, 0:4, HALF:], bank(("gather_over", l, 0))[:].rearrange("p (c n) -> p c n", c=4)),
                     ("gather_over", l, 0))
                ready(act, ("slotsT", l, 0))
                free(copy(slots_T[:, 0:2, :], bank(("slotsT", l, 0))[:].rearrange("p (c n) -> p c n", c=2)),
                     ("slotsT", l, 0))

                def step(i):
                    for e in range(PER_GROUP):
                        ready(act, ("gate", l, e), i)
                        free(s.activation(sg[:, e % 2, :], bank(("gate", l, e))[:], ACT.Silu), ("gate", l, e))
                        ready(act, ("hT", l, e), i)
                        free(copy(hxT[:, e % 2, :, :], bank(("hT", l, e))[:].rearrange("p (j n) -> p j n", j=4)),
                             ("hT", l, e))
                    ready(act, ("y", l, 0), i)
                    free(copy(y_sb[:, bass.ds(i, 1), 0:HALF].rearrange("p o n -> p (o n)"), bank(("y", l, 0))[:]),
                         ("y", l, 0))
                more = spilled(act, l)
                with act.Fori(0, GROUPS) as i:
                    step(i)
                with act.If(more > 0):
                    step(GROUPS)
                with act.Else():
                    skipped(act, bank_free, [("gate", l, 2), ("gate", l, 3), ("hT", l, 2), ("hT", l, 3), ("y", l, 0)])

            std("ln0", eps_ln)
            evac_T("ln0", xT, R_MIXG, R_MIXB)
            act.wait_ge(sem("biases"), 16)
            experts(0)
            std("ln1", eps_ln)
            evac_T("ln1", xT, R_FFNG, R_FFNB)
            for name, dst in (("k", kT), ("q", qT)):
                for n in range(0, KD, 2):
                    ready(act, (name, n))
                    free(copy(dst[:, n, :], bank((name, n))[:, 0:T]), (name, n))
            for half in range(2):
                ready(act, ("v", half, 0))
                free(copy(vtok[:, 0, half * HALF:(half + 1) * HALF], bank(("v", half, 0))[:]), ("v", half, 0))
            act.wait_ge(sem("lam_dot"), 1)
            s.activation(lam[:, 2:4], lam[:, 0:2], ACT.Exp).then_inc(sem("lam_exp"), 1)

            def weights(u):
                qt, h = units[u]
                n = (qt + 1) * P
                act.wait_ge(sem("dmax"), u + 1)
                for m in range(2):
                    s.activation(prob[:, u % 2, m, 0:n], logit[:, u % 2, m, 0:n], ACT.Exp,
                                 bias=dneg[:, u % 2, m:m + 1], accum_out=dsum[:, u % 2, m:m + 1])\
                     .then_inc(sem("dexp"), 1)

            def weights_T(u):
                qt, h = units[u]
                ready(act, ("pT", u))
                free(copy(diffT[:, u % 2, 0:qt + 1, :],
                          bank(("pT", u))[:, 0:(qt + 1) * P].rearrange("p (k n) -> p k n", n=P)), ("pT", u))
            for u in range(len(units)):
                weights(u)
                if u:
                    weights_T(u - 1)
            weights_T(len(units) - 1)
            for t in range(NT):
                act.wait_ge(sem("oms"), t + 1)
                s.activation(ostd[:, t, :], oms[:, t, :], ACT.Sqrt, scale=1.0 / VD, bias=eps_ln[:])\
                 .then_inc(sem("ostd"), 1)
            evac_T("o", xT)
            std("ln2", eps_ln)
            evac_T("ln2", xT, R_MIXG + KD, R_MIXB + KD)
            experts(1)
            std("ln3", eps_ln)

            def mean_square(n, arrived, of):
                for t in range(NT):
                    act.wait_ge(sem(arrived), of[t])
                    s.activation(res[:, t, :], xtok[:, t, :], ACT.Square, accum_out=mv[:, t, 0:1])\
                     .then_inc(sem(f"{n}_sq"), 1)
                for t in range(NT):
                    act.wait_ge(sem(f"{n}_sq"), t + 1)
                    s.activation(rstd[:, t, 0:1], mv[:, t, 0:1], ACT.Sqrt, scale=1.0 / D, bias=eps_rms[:])\
                     .then_inc(sem(f"{n}_std"), 1)
            mean_square("rm0", "ln3_tok", (1, 2))
            evac_T("rm0", xT, R_MIX2)
            for t in range(NT):
                ready(act, ("akv", t))
                free(copy(akv[:, t, :], bank(("akv", t))[:]), ("akv", t))
            act.wait_ge(sem("qk_ms"), 1)
            s.activation(qkstd, qkms, ACT.Sqrt, scale=1.0 / HD, bias=eps_rms[:]).then_inc(sem("qk_std"), 1)
            for n in range(4):
                ready(act, ("hf", n))
                free(copy(zf[:, n, :], bank(("hf", n))[:, 0:T]), ("hf", n))
            for n in range(4):
                ready(act, ("hq", n))
                free(copy(qh[:, n, :], bank(("hq", n))[:, 0:T]), ("hq", n))
            ready(act, ("hi", 0))
            free(copy(itok[:, 0, :], bank(("hi", 0))[:]), ("hi", 0))
            ready(act, ("qaT", 0))
            free(copy(qaT[:, 0:2, :], bank(("qaT", 0))[:].rearrange("p (c t) -> p c t", c=2)), ("qaT", 0))
            ready(act, "kaT")
            free(copy(kaT, bank("kaT")[:].rearrange("p (c t) -> p c t", c=2)), "kaT")
            ready(act, "ikT")
            free(copy(ikT, bank("ikT")[:, 0:T]), "ikT")
            freed(act, ("hf", 3))
            s.activation(ez, zf, ACT.Abs).then_inc(sem("hz"), 1)
            act.wait_ge(sem("hz"), 1)
            s.activation(ez, ez, ACT.Exp, scale=-1.0).then_inc(sem("hz"), 1)
            act.wait_ge(sem("hz"), 2)
            s.activation(ez, ez, ACT.Ln, bias=one1[:]).then_inc(sem("hz"), 1)
            s.activation(kk, zf, ACT.Sigmoid, scale=-1.0).then_inc(sem("hk"), 1)
            for qt in range(NT):
                n = (qt + 1) * P
                for b in range(2):
                    ready(act, ("is", qt, b))
                    if qt:
                        act.wait_ge(sem("isc"), qt)
                    for j in range(2):
                        last = s.activation(relus[:, 2 * j + b, 0:n], bank(("is", qt, b))[:, j * T:j * T + n], ACT.Relu)
                    free(last, ("is", qt, b))
            for name, dst in (("cc", cc), ("cb", cb)):
                for n in range(4):
                    ready(act, (name, n))
                    free(copy(dst[:, n, :], bank((name, n))[:, 0:T]), (name, n))

            def weights2(qt, u):
                n = (qt + 1) * P
                k = qt * 4 + u
                act.wait_ge(sem("amax"), k + 1)
                for j in range(2):
                    s.activation(s2[:, u % 2, j, 0:n], s2[:, u % 2, j, 0:n], ACT.Exp,
                                 bias=aneg[:, u % 2, j:j + 1],
                                 accum_out=asum[:, qt, unit_heads(u)[j]:unit_heads(u)[j] + 1]).then_inc(sem("aexp"), 1)

            def weights2_T(qt, u):
                ready(act, ("p2T", qt, u, 0))
                free(copy(pT2[:, 0, 0:qt + 1, :],
                          bank(("p2T", qt, u, 0))[:, 0:(qt + 1) * P].rearrange("p (k n) -> p k n", n=P)),
                     ("p2T", qt, u, 0))
            for qt in range(NT):
                for u in range(4):
                    weights2(qt, u)
                    if u or qt:
                        k = qt * 4 + u - 1
                        weights2_T(k // 4, k % 4)
            weights2_T(1, 3)
            ready(act, ("yaT", 0))
            free(copy(yaT[:, 0:2, :], bank(("yaT", 0))[:].rearrange("p (c t) -> p c t", c=2)), ("yaT", 0))
            freed(act, ("yaT", 1))
            for n in range(len(LEVELS) + 1):
                act.wait_ge(sem("hdiff"), n + 1)
                s.activation(ez, ez, ACT.Exp).then_inc(sem("hdecay"), 1)
                for t in range(NT if n in BETWEEN else 0):
                    use_ = (*BETWEEN[n], t)
                    ready(act, use_)
                    if n == 0:
                        free(s.activation(hgs[:, t, :], bank(use_)[:], ACT.Silu), use_)
                    else:
                        free(s.activation(gates[:, BETWEEN[n][1], t, :], bank(use_)[:], ACT.Sigmoid), use_)
            ready(act, "lev01")
            free(copy(att01, bank("lev01")[:].rearrange("p (h t) -> p h t", h=HH)), "lev01")
            for t in range(NT):
                act.wait_ge(sem("hms"), t + 1)
                s.activation(hstd[:, t, :], hms[:, t, :], ACT.Sqrt, scale=1.0 / VD, bias=eps_rms[:])\
                 .then_inc(sem("hstd"), 1)
            ready(act, ("yhT", 0))
            free(copy(yhT[:, 0:2, :], bank(("yhT", 0))[:].rearrange("p (c t) -> p c t", c=2)), ("yhT", 0))
            evac_T("mixed", xT)
            mean_square("rm1", "mixed_in", (1, 2))
            evac_T("rm1", xT, R_MLP2)
            with act.Fori(0, 4) as i:
                for j in range(2):
                    for t in range(NT):
                        ready(act, ("mu", j, t), i)
                        free(s.activation(mr[:, j, t, :], bank(("mu", j, t))[:], ACT.Relu), ("mu", j, t))
                    ready(act, ("mT", j, 0), i)
                    free(copy(mhT[:, j, :, 0:P], bank(("mT", j, 0))[:].rearrange("p (c n) -> p c n", c=4)),
                         ("mT", j, 0))


        CONSTS = 9
        NORMS = {"ln0": 0, "ln1": 1, "ln2": 2, "ln3": 3}

        @blk.tensor
        def _(pe):
            mm, tr = nc.tensor.matmul, nc.tensor.transpose

            def transposes(name, src):
                for b in range(4):
                    claim(pe, (name, b))
                    for c in (2 * b, 2 * b + 1):
                        for t in range(NT):
                            at = c % 2 * T + t * P
                            last = tr(bank((name, b))[:, at:at + P], src[:, t, c * P:(c + 1) * P], ident[:])
                    full(last, (name, b))

            def have_T(name):
                for b in range(4):
                    freed(pe, (name, b))

            def linear_tok(name, label, cols=HALF, src=xT, bias=None):
                for t in range(NT):
                    use_ = (*name, t) if isinstance(name, tuple) else (name, t)
                    claim(pe, use_)
                    landed(pe, label)
                    for k in range(KD):
                        last = mm(bank(use_)[:, 0:cols], src[:, k, t * P:(t + 1) * P], block(label)[:, k, :],
                                  start=k == 0, stop=k == KD - 1 and bias is None)
                    if bias is not None:
                        last = mm(bank(use_)[:, 0:cols], ones[0:1, :], bias, start=False, stop=True)
                    full(last, use_)

            def linear_T(name, label, n0=0):
                for n in range(4):
                    claim(pe, (name, n0 + n))
                    landed(pe, label)
                    for k in range(KD):
                        last = mm(bank((name, n0 + n))[:, 0:T], block(label)[:, k, n * P:(n + 1) * P], xT[:, k, :],
                                  start=k == 0, stop=k == KD - 1)
                    full(last, (name, n0 + n))

            pe.wait_ge(sem("ident"), 1)
            pe.wait_ge(sem("x_in"), 16)
            transposes("x", xtok)

            def glu_T(half):
                pe.wait_ge(sem("glu"), (half + 1) * NT)
                for b in range(2):
                    claim(pe, ("glu", half, b))
                    for j in range(2):
                        c = 4 * half + 2 * b + j
                        for t in range(NT):
                            last = tr(bank(("glu", half, b))[:, j * T + t * P:j * T + (t + 1) * P],
                                      glu[:, t, c * P:(c + 1) * P], ident[:])
                    full(last, ("glu", half, b))
            def pw1(kind, half):
                c0 = (D if kind == "g" else 0) + half * HALF
                linear_tok(("pw1", kind, half), ("pw1", kind, half), bias=b1row[0:1, c0:c0 + HALF])
            have_T("x")
            pe.wait_ge(sem("c0"), 2)
            pe.wait_ge(sem("par_b1"), 16)
            pw1("a", 0)
            pw1("g", 0)
            pe.wait_ge(sem("par_rows"), 16 * 10)
            claim(pe, "params")
            full(tr(bank("params")[:, 0:R_ROWS], params[0:R_ROWS, :], ident[0:R_ROWS, 0:R_ROWS]), "params")
            pe.wait_ge(sem("par_taps"), 16 * 2)
            claim(pe, "taps")
            for n in range(2):
                last = tr(bank("taps")[:, n * 124:(n + 1) * 124], wst[0:124, n, :], ident[0:124, 0:124])
            full(last, "taps")
            pe.wait_ge(sem("consts"), CONSTS)
            pe.wait_ge(sem("table_ahead"), 1)
            pe.wait_ge(sem("par_tables"), 16 * 3)
            claim(pe, "line")
            full(mm(bank("line")[0:2 * HEADS, :], tables[:], onehot[0:33, :], start=True, stop=True), "line")
            pw1("a", 1)
            glu_T(0)
            pw1("g", 1)
            glu_T(1)

            def taps(j, start=False, stop=False):
                for n, c in enumerate(PE_CHUNKS):
                    pe.wait_ge(sem(f"diag{n}"), j + 1)
                    ins = mm(bank(("tap", c))[:, 0:T], diag[:, n, :], hpad[:, c, bass.ds(j, T)], start=start, stop=stop)
                    if stop:
                        full(ins, ("tap", c))
                    else:
                        ins.then_inc(sem(f"diag{n}_read"), 1)
            for b in range(2):
                freed(pe, ("glu", 1, b))
            for c in PE_CHUNKS:
                claim(pe, ("tap", c))
            taps(0, start=True)
            with pe.Fori(1, CONV - 1) as j:
                taps(j)
            taps(CONV - 1, stop=True)
            for n, group in enumerate(DVE_CHUNKS):
                pe.wait_ge(sem(f"conv{n}"), CONV * len(group))
            for c in PE_CHUNKS:
                freed(pe, ("tap", c))
            for name, src, signal in (("conv_mean", conv, None), ("conv_var", squares, "conv_sq")):
                if signal:
                    pe.wait_ge(sem(signal), 1)
                claim(pe, name)
                for k in range(KD):
                    last = mm(bank(name)[:, 0:T], mean_w[:], src[:, k, :], start=k == 0, stop=k == KD - 1)
                full(last, name)
            pe.wait_ge(sem("reverse"), 2)
            pe.wait_ge(sem("shifted"), 32)
            for table in range(2):
                for q in range(4):
                    claim(pe, ("bias", table, q))
                    full(mm(bank(("bias", table, q))[:], reverse, shifted[:, table, q * HALF:(q + 1) * HALF],
                            start=True, stop=True), ("bias", table, q))
            pe.wait_ge(sem("conv_silu"), KD)
            for half in range(2):
                linear_tok(("pw2", half), ("pw2", half))

            def norm_T(name):
                pe.wait_ge(sem(f"{name}_xhat"), NT)
                transposes(name, res)
                have_T(name)

            def experts(l):
                n = f"ln{2 * l}"
                claim(pe, ("router", l))
                pe.wait_ge(sem("par_router"), 32)
                for t in range(NT):
                    for k in range(KD):
                        last = mm(bank(("router", l))[:, t * EXPERTS:(t + 1) * EXPERTS], xT[:, k, t * P:(t + 1) * P],
                                  rw[:, k, :], start=k == 0, stop=k == KD - 1)
                full(last, ("router", l))
                claim(pe, ("rank", l))
                pe.wait_ge(sem(f"in_group{l}"), 1)
                r = bank(("rank", l))
                mm(r[:, 0:4], earlier[:], in_group[:, 0, :], start=True, stop=True)
                mm(r[:, 4:8], ones[:], in_group[:, 0, :], start=True, stop=False)
                mm(r[:, 4:8], earlier[:], in_group[:, 1, :], start=False, stop=True)
                mm(r[:, 8:12], ones[:], in_group[:, 0, :], start=True, stop=False)
                full(mm(r[:, 8:12], ones[:], in_group[:, 1, :], start=False, stop=True), ("rank", l))
                pe.wait_ge(sem(f"slots{l}"), NT)
                pe.wait_ge(sem(f"{n}_tok"), 2)
                for c in range(KD):
                    claim(pe, ("gather", l, c))
                    for t in range(NT):
                        last = mm(bank(("gather", l, c))[:], xtok[:, t, c * P:(c + 1) * P], sel_slots[:, t, 0:HALF],
                                  start=t == 0, stop=t == NT - 1)
                    full(last, ("gather", l, c))
                for b in range(2):
                    claim(pe, ("gather_over", l, b))
                    for c in range(4):
                        for t in range(NT):
                            last = mm(bank(("gather_over", l, b))[:, c * P:(c + 1) * P],
                                      xtok[:, t, (4 * b + c) * P:(4 * b + c + 1) * P], sel_slots[:, t, HALF:],
                                      start=t == 0, stop=t == NT - 1)
                    full(last, ("gather_over", l, b))
                for b in range(3):
                    claim(pe, ("slotsT", l, b))
                    for st in range(2 * b, min(2 * b + 2, STEPS)):
                        for t in range(NT):
                            last = tr(bank(("slotsT", l, b))[:, st % 2 * T + t * P:st % 2 * T + (t + 1) * P],
                                      sel_slots[:, t, st * P:(st + 1) * P], ident[:])
                    full(last, ("slotsT", l, b))
                claim(pe, ("slot_gates", l))
                pe.wait_ge(sem(f"gates4_{l}"), 1)
                for st in range(STEPS):
                    for t in range(NT):
                        last = mm(bank(("slot_gates", l))[:, st * PER_GROUP:(st + 1) * PER_GROUP],
                                  sel_slots[:, t, st * P:(st + 1) * P], gates4[:, t, :], start=t == 0, stop=t == NT - 1)
                full(last, ("slot_gates", l))

                def step(i):
                    def into(kind, e):
                        claim(pe, (kind, l, e), i)
                        landed(pe, (kind, l, e), i)
                        for k in range(KD):
                            last = mm(bank((kind, l, e))[:], xg[:, k, :], block((kind, l, e))[:, k, :],
                                      start=k == 0, stop=k == KD - 1)
                        full(last, (kind, l, e))

                    def hidden_T(e):
                        claim(pe, ("hT", l, e), i)
                        freed(pe, ("up", l, e), i)
                        for j in range(4):
                            last = tr(bank(("hT", l, e))[:, j * P:(j + 1) * P], hx[:, e % 2, j * P:(j + 1) * P], ident[:])
                        full(last, ("hT", l, e))

                    def down(e):
                        if e == 0:
                            for h in range(2):
                                claim(pe, ("y", l, h), i)
                        freed(pe, ("hT", l, e), i)
                        landed(pe, ("down", l, e), i)
                        for h in range(2):
                            for j in range(4):
                                last = mm(bank(("y", l, h))[:], hxT[:, e % 2, j, :],
                                          block(("down", l, e))[:, j, h * HALF:(h + 1) * HALF],
                                          start=e == 0 and j == 0, stop=e == PER_GROUP - 1 and j == 3)
                            if e == PER_GROUP - 1:
                                full(last, ("y", l, h))
                        if e < PER_GROUP - 1:
                            last.then_inc(sem(f"down_read{l}"), 1)
                    pe.wait_ge(sem(f"xg{l}"), i + 1)
                    for e in range(PER_GROUP):
                        into("gate", e)
                        if e:
                            hidden_T(e - 1)
                        into("up", e)
                        if e:
                            down(e - 1)
                    hidden_T(PER_GROUP - 1)
                    down(PER_GROUP - 1)
                more = spilled(pe, l)
                with pe.Fori(0, GROUPS) as i:
                    step(i)
                with pe.If(more > 0):
                    step(GROUPS)
                with pe.Else():
                    skipped(pe, bank_ready, [("gate", l, 2), ("gate", l, 3), ("up", l, 2), ("up", l, 3), ("hT", l, 2),
                                             ("hT", l, 3), ("y", l, 0), ("y", l, 1)])
                    pe.wait_ge(sem(f"down_read{l}"), (PER_GROUP - 1) * GROUPS)
                    pe.sem_inc(sem(f"down_read{l}"), PER_GROUP - 1)
                for b in range(3):
                    freed(pe, ("slotsT", l, b))
                for h in range(2):
                    freed(pe, ("y", l, h), STEPS - 1)
                for t in range(NT):
                    for h in range(2):
                        claim(pe, ("scatter", l, t, h))
                        for st in range(STEPS):
                            last = mm(bank(("scatter", l, t, h))[:], slots_T[:, st, t * P:(t + 1) * P],
                                      y_sb[:, st, h * HALF:(h + 1) * HALF], start=st == 0, stop=st == STEPS - 1)
                        full(last, ("scatter", l, t, h))

            norm_T("ln0")
            experts(0)
            norm_T("ln1")
            for name in ("k", "q"):
                for half in range(2):
                    linear_T(name, (name, half), 4 * half)
            for half in range(2):
                linear_tok(("v", half), ("v", half))
            for name in ("k", "q"):
                for n in range(4, KD):
                    freed(pe, (name, n))
            for half in range(2):
                for t in range(NT):
                    freed(pe, ("v", half, t))

            def scores(u):
                qt, h = units[u]
                claim(pe, ("s", u))
                n, d0 = (qt + 1) * P, h % 2 * HD
                for m in range(2):
                    c = m * 4 + h // 2
                    last = mm(bank(("s", u))[:, m * T:m * T + n], qT[d0:d0 + HD, c, qt * P:(qt + 1) * P],
                              kT[d0:d0 + HD, c, 0:n], start=True, stop=True)
                full(last, ("s", u))
            scores(0)
            scores(1)
            for u, (qt, h) in enumerate(units):
                claim(pe, ("pT", u))
                pe.wait_ge(sem("diffp"), u + 1)
                for kt in range(qt + 1):
                    last = tr(bank(("pT", u))[:, kt * P:(kt + 1) * P], diffp[:, u % 2, kt * P:(kt + 1) * P], ident[:])
                full(last, ("pT", u))
                if u + 2 < len(units):
                    scores(u + 2)
                o = ("o", qt, h // 4)
                if h % 4 == 0:
                    claim(pe, o)
                freed(pe, ("pT", u))
                for kt in range(qt + 1):
                    last = mm(bank(o)[:, h % 4 * VD:(h % 4 + 1) * VD], diffT[:, u % 2, kt, :],
                              vtok[:, kt, h * VD:(h + 1) * VD], start=kt == 0, stop=kt == qt)
                if h % 4 == 3:
                    full(last, o)
            pe.wait_ge(sem("onorm"), NT)
            transposes("o", otok)
            have_T("o")
            for half in range(2):
                linear_tok(("wo", half), ("wo", half))
            norm_T("ln2")
            experts(1)

            norm_T("rm0")
            linear_tok("ikw", "ikw", IKW)
            linear_tok("akv", "akv")
            linear_tok("aq", "aq")
            linear_T("hf", "hf")
            linear_T("hq", "hq")
            linear_tok("hi", "hi")
            pe.wait_ge(sem("qk_norm"), 1)

            def pieces(label, srcs):
                claim(pe, label)
                for j, src in enumerate(srcs):
                    for t in range(NT):
                        last = tr(bank(label)[:, j * T + t * P:j * T + (t + 1) * P], src(t), ident[:])
                full(last, label)
            for b in range(2):
                pieces(("qaT", b), [lambda t, c=2 * b + j: aq[:, t, c * P:(c + 1) * P] for j in range(2)])
            pieces("kaT", [lambda t, g=g: kd[:, t, g, :] for g in range(2)])
            pieces("iqT", [lambda t, j=j: akv[:, t, 2 * P + j * P:2 * P + (j + 1) * P] for j in range(2)])
            pieces("ikT", [lambda t: ikd[:, t, :]])
            for label in ("iqT", "ikT"):
                freed(pe, label)
            for qt in range(NT):
                n = (qt + 1) * P
                for b in range(2):
                    claim(pe, ("is", qt, b))
                    for j in range(2):
                        d0 = b * HD
                        last = mm(bank(("is", qt, b))[:, j * T:j * T + n], iqT[d0:d0 + HD, j, qt * P:(qt + 1) * P],
                                  ikT[d0:d0 + HD, 0:n], start=True, stop=True)
                    full(last, ("is", qt, b))
            for name in ("cc", "ch", "cb"):
                linear_T(name, name)
            for label in (("qaT", 0), ("qaT", 1), "kaT"):
                freed(pe, label)

            def scores2(k):
                qt, u = k // 4, k % 4
                n = (qt + 1) * P
                claim(pe, ("s2", qt, u))
                for j in range(2):
                    d0, c = u % 2 * HD, u // 2 * 2 + j
                    last = mm(bank(("s2", qt, u))[:, j * T:j * T + n], qaT[d0:d0 + HD, c, qt * P:(qt + 1) * P],
                              kaT[d0:d0 + HD, u // 2, 0:n], start=True, stop=True)
                full(last, ("s2", qt, u))
            scores2(0)
            scores2(1)
            for k in range(8):
                qt, u = k // 4, k % 4
                for j in range(2):
                    claim(pe, ("p2T", qt, u, j))
                    pe.wait_ge(sem("aexp"), 2 * k + j + 1)
                    for kt in range(qt + 1):
                        last = tr(bank(("p2T", qt, u, j))[:, kt * P:(kt + 1) * P], s2[:, u % 2, j, kt * P:(kt + 1) * P],
                                  ident[:])
                    full(last, ("p2T", qt, u, j))
                if k + 2 < 8:
                    scores2(k + 2)
                if u == 0:
                    claim(pe, ("o2", qt))
                for j in range(2):
                    freed(pe, ("p2T", qt, u, j))
                    h = unit_heads(u)[j]
                    v0 = P + u // 2 * HD
                    for kt in range(qt + 1):
                        last = mm(bank(("o2", qt))[:, h * HD:(h + 1) * HD], pT2[:, j, kt, :], akv[:, kt, v0:v0 + HD],
                                  start=kt == 0, stop=kt == qt)
                if u == 3:
                    full(last, ("o2", qt))
            for qt in range(NT):
                freed(pe, ("o2", qt))
            for b in range(2):
                pieces(("yaT", b), [lambda t, c=2 * b + j: yat[:, t, c * P:(c + 1) * P] for j in range(2)])

            for n in range(len(LEVELS) + 1):
                q_, k_ = (qh, kk) if n == 0 else (qe, ke)
                pe.wait_ge(sem("hqk"), n + 1)
                for t in range(NT):
                    claim(pe, ("lev", n, t))
                    for h in range(HH):
                        last = mm(bank(("lev", n, t))[:, h * P:(h + 1) * P], k_[:, h, t * P:(t + 1) * P],
                                  q_[:, h, t * P:(t + 1) * P], start=True, stop=True)
                    full(last, ("lev", n, t))
                if n in BETWEEN:
                    linear_tok(BETWEEN[n], BETWEEN[n] if len(BETWEEN[n]) > 1 else BETWEEN[n][0])
            claim(pe, "lev01")
            pe.wait_ge(sem("hqk"), len(LEVELS) + 2)
            for h in range(HH):
                last = mm(bank("lev01")[:, h * P:(h + 1) * P], ke[:, h, 0:P], qe[:, h, P:T], start=True, stop=True)
            full(last, "lev01")
            freed(pe, "lev01")
            for t in range(NT):
                claim(pe, ("oh", t))
                pe.wait_ge(sem("att"), t + 1)
                for h in range(HH):
                    o = bank(("oh", t))[:, h * P:(h + 1) * P]
                    if t:
                        mm(o, att01[:, h, :], itok[:, 0, h * P:(h + 1) * P], start=True, stop=False)
                    last = mm(o, attT[:, t, h, :], itok[:, t, h * P:(h + 1) * P], start=t == 0, stop=True)
                full(last, ("oh", t))
            pe.wait_ge(sem("yh"), NT)
            for b in range(2):
                pieces(("yhT", b), [lambda t, c=2 * b + j: yh[:, t, c * P:(c + 1) * P] for j in range(2)])
            for b in range(2):
                freed(pe, ("yaT", b))
                freed(pe, ("yhT", b))
            pe.wait_ge(sem("yc"), 1)
            for br, src in enumerate((yaT, yhT, ycT)):
                landed(pe, ("branch", br))
                for t in range(NT):
                    for h in range(2):
                        claim(pe, ("branch", br, t, h))
                        for k in range(4):
                            last = mm(bank(("branch", br, t, h))[:], src[:, k, t * P:(t + 1) * P],
                                      block(("branch", br))[:, k, h * HALF:(h + 1) * HALF], start=k == 0, stop=k == 3)
                        full(last, ("branch", br, t, h))
            pe.wait_ge(sem("mixed"), 1)
            transposes("mixed", mixed)
            have_T("mixed")
            for h in range(2):
                linear_tok(("out", h), ("out", h))
            norm_T("rm1")

            def mlp(i, first=False, last_=False):
                for j in range(2):
                    for t in range(NT):
                        claim(pe, ("mu", j, t), i)
                        landed(pe, ("mu", j), i)
                        for k in range(KD):
                            last = mm(bank(("mu", j, t))[:], xT[:, k, t * P:(t + 1) * P], block(("mu", j))[:, k, :],
                                      start=k == 0, stop=k == KD - 1)
                        full(last, ("mu", j, t))
                for j in range(2):
                    for t in range(NT):
                        claim(pe, ("mT", j, t), i)
                        pe.wait_ge(sem("mh"), 4 * i + 2 * j + t + 1)
                        for c in range(4):
                            last = tr(bank(("mT", j, t))[:, c * P:(c + 1) * P], mh[:, j, t, c * P:(c + 1) * P], ident[:])
                        full(last, ("mT", j, t))
                    landed(pe, ("md", j), i)
                    for t in range(NT):
                        freed(pe, ("mT", j, t), i)
                        for h in range(2):
                            if first and j == 0:
                                claim(pe, ("md", t, h))
                            for k in range(4):
                                last = mm(bank(("md", t, h))[:], mhT[:, j, k, t * P:(t + 1) * P],
                                          block(("md", j))[:, k, h * HALF:(h + 1) * HALF],
                                          start=first and j == 0 and k == 0, stop=last_ and j == 1 and k == 3)
                    last.then_inc(sem("md_read"), 1)
            mlp(0, first=True)
            with pe.Fori(1, 3) as i:
                mlp(i)
            mlp(3, last_=True)

        @blk.vector
        def _(dve):
            v = nc.vector
            chain = [0]

            def link(ins):
                chain[0] += 1
                ins.then_inc(sem("dve_chain"), 1)
                dve.wait_ge(sem("dve_chain"), chain[0])

            def evac_T(name, dst, gain=None, shift=None):
                for b in (1, 3):
                    ready(dve, (name, b))
                    for c in (2 * b, 2 * b + 1):
                        src = bank((name, b))[:, c % 2 * T:c % 2 * T + T]
                        if gain is None:
                            last = v.tensor_copy(dst[:, c, :], src)
                        elif shift is None:
                            last = v.tensor_scalar(dst[:, c, :], src, pcol[:, gain + c:gain + c + 1], None, ALU.mult)
                        else:
                            last = v.tensor_scalar(dst[:, c, :], src, pcol[:, gain + c:gain + c + 1],
                                                   pcol[:, shift + c:shift + c + 1], ALU.mult, ALU.add)
                    free(last, (name, b))

            def bcast(x, *shape):
                return x.broadcast_to([P, *shape])

            v.memset(tables[32:33, :], MASKED).then_inc(sem("table_ahead"), 1)
            evac_T("x", xT)
            ready(dve, ("glu", 0, 1))
            dve.wait_ge(sem("hpad0"), 1)
            for j in range(2):
                last = v.tensor_copy(hpad[:, 2 + j, CONV - 1:], bank(("glu", 0, 1))[:, j * T:(j + 1) * T])
            free(last, ("glu", 0, 1))
            freed(dve, "params")
            freed(dve, "taps")
            for n, group in enumerate(DVE_CHUNKS):
                for b in range(2):
                    freed(dve, ("glu", n, b))
                for c in group:
                    v.tensor_scalar(conv[:, c, :], hpad[:, c, 0:T], wdw[:, c:c + 1], pcol[:, R_BDW + c:R_BDW + c + 1],
                                    ALU.mult, ALU.add).then_inc(sem(f"conv{n}"), 1)
                with dve.Fori(1, CONV) as j:
                    for k, c in enumerate(group):
                        dve.wait_ge(sem(f"conv{n}"), (j - 1) * len(group) + k + 1)
                        v.scalar_tensor_tensor(conv[:, c, :], hpad[:, c, bass.ds(j, T)], wdw[:, bass.ds(j * KD + c, 1)],
                                               conv[:, c, :], ALU.mult, ALU.add).then_inc(sem(f"conv{n}"), 1)
            ready(dve, "conv_mean")
            for n, group in enumerate(DVE_CHUNKS):
                dve.wait_ge(sem(f"conv{n}"), CONV * len(group))
            for c in PE_CHUNKS:
                freed(dve, ("tap", c))
            free(v.tensor_tensor(conv, conv, bcast(bank("conv_mean")[:, 0:T].unsqueeze(1), KD, T), ALU.subtract),
                 "conv_mean")
            freed(dve, "conv_var")
            link(v.reciprocal(cstd[:, 1, :], cstd[:, 0, :]))
            v.tensor_tensor(conv, conv, bcast(cstd[:, 1:2, :], KD, T), ALU.mult).then_inc(sem("conv_normal"), 1)
            for table in range(2):
                for q in range(4):
                    ready(dve, ("bias", table, q))
                    free(v.tensor_copy(shifted[:, table, q * HALF:(q + 1) * HALF], bank(("bias", table, q))[:]),
                         ("bias", table, q))
            dve.wait_ge(sem("par_b2"), 16)
            link(v.scalar_tensor_tensor(res[:], xtok[:], ALPHA, bcast(b2row.unsqueeze(1), NT, D), ALU.mult, ALU.add))
            for half in range(2):
                for t in range(NT):
                    ready(dve, ("pw2", half, t))
                    r = res[:, t, half * HALF:(half + 1) * HALF]
                    free(v.tensor_tensor(r, r, bank(("pw2", half, t))[:], ALU.add), ("pw2", half, t))

            def layer_norm(n):
                for t in range(NT):
                    for h in range(2):
                        ins = v.bn_stats(stats[:, t, h, :], res[:, t, h * HALF:(h + 1) * HALF])
                    link(ins)
                    v.bn_aggr(mv[:, t, :], stats[:, t, :, :]).then_inc(sem(f"{n}_var"), 1)
                for t in range(NT):
                    dve.wait_ge(sem(f"{n}_std"), t + 1)
                    link(v.reciprocal(rstd[:, t, 1:2], rstd[:, t, 0:1]))
                    v.tensor_scalar(res[:, t, :], res[:, t, :], mv[:, t, 0:1], rstd[:, t, 1:2], ALU.subtract, ALU.mult)\
                        .then_inc(sem(f"{n}_xhat"), 1)

            def rms_norm(n):
                for t in range(NT):
                    dve.wait_ge(sem(f"{n}_std"), t + 1)
                    link(v.reciprocal(rstd[:, t, 1:2], rstd[:, t, 0:1]))
                    v.tensor_scalar(res[:, t, :], xtok[:, t, :], rstd[:, t, 1:2], None, ALU.mult)\
                        .then_inc(sem(f"{n}_xhat"), 1)

            def experts(l):
                freed(dve, ("router", l))
                if l == 0:
                    dve.wait_ge(sem("par_router"), 32)
                    dve.wait_ge(sem("consts"), CONSTS)
                link(v.tensor_tensor(sel.rearrange("p (t g) e -> p t (g e)", t=NT), aff,
                                     bcast(rbias[:].unsqueeze(1), NT, EXPERTS), ALU.add))
                v.tensor_tensor(pair_hi, sel[:, :, 0::2], sel[:, :, 1::2], ALU.max)
                link(v.tensor_tensor(pair_lo, sel[:, :, 0::2], sel[:, :, 1::2], ALU.min))
                v.tensor_tensor(top[:, 0, :], pair_hi[:, :, 0], pair_hi[:, :, 1], ALU.max)
                v.tensor_tensor(top[:, 1, :], pair_hi[:, :, 0], pair_hi[:, :, 1], ALU.min)
                link(v.tensor_tensor(top[:, 2, :], pair_lo[:, :, 0], pair_lo[:, :, 1], ALU.max))
                link(v.tensor_tensor(top[:, 1, :], top[:, 1, :], top[:, 2, :], ALU.max))
                link(v.tensor_tensor(gscore.rearrange("p t g -> p (t g)"), top[:, 0, :], top[:, 1, :], ALU.add))
                link(v.tensor_reduce(gbest, gscore, AX, ALU.max))
                link(v.tensor_tensor(gkey, gscore, bcast(gbest.unsqueeze(2), NT, GROUPS), ALU.is_equal))
                link(v.tensor_tensor(gkey, gkey, bcast(first_g[:].unsqueeze(1), NT, GROUPS), ALU.mult))
                link(v.tensor_reduce(gbest, gkey, AX, ALU.max))
                v.tensor_tensor(in_group, gkey, bcast(gbest.unsqueeze(2), NT, GROUPS), ALU.is_equal)\
                    .then_inc(sem(f"in_group{l}"), 1)
                dve.wait_ge(sem(f"in_group{l}"), 1)
                se = bcast(sel.unsqueeze(3), NG, PER_GROUP, PER_GROUP)
                sj = bcast(sel.unsqueeze(2), NG, PER_GROUP, PER_GROUP)
                v.tensor_tensor(beats, sj, se, ALU.is_gt)
                link(v.tensor_tensor(ties, sj, se, ALU.is_equal))
                link(v.tensor_tensor(ties, ties, bcast(lower_e[:].unsqueeze(1), NG, PER_GROUP, PER_GROUP), ALU.mult))
                link(v.tensor_tensor(beats, beats, ties, ALU.add))
                link(v.tensor_reduce(place, beats, AX, ALU.add))
                link(v.tensor_scalar(place, place, 1.5, None, ALU.is_lt))
                link(v.tensor_tensor(place, place, bcast(in_group.rearrange("p t g -> p (t g)").unsqueeze(2), NG, PER_GROUP),
                                     ALU.mult))
                link(v.tensor_tensor(place, place, aff.rearrange("p t (g e) -> p (t g) e", g=GROUPS), ALU.mult))
                link(v.tensor_reduce(gates4, place.rearrange("p (t g) e -> p t e g", t=NT), AX, ALU.add))
                link(v.tensor_reduce(gsum, gates4, AX, ALU.add))
                link(v.reciprocal(gsum, gsum))
                v.tensor_tensor(gates4, gates4, bcast(gsum.unsqueeze(2), NT, PER_GROUP), ALU.mult)\
                    .then_inc(sem(f"gates4_{l}"), 1)
                ready(dve, ("rank", l))
                r = bank(("rank", l))
                link(v.tensor_tensor(pos, in_group, r[:, 0:2 * GROUPS].rearrange("p (t g) -> p t g", t=NT), ALU.mult))
                link(v.tensor_reduce(slot[:, 0, :], pos, AX, ALU.add))
                link(v.tensor_tensor(pos, in_group, bcast(index_g[:].unsqueeze(1), NT, GROUPS), ALU.mult))
                link(v.tensor_reduce(slot[:, 1, :], pos, AX, ALU.add))
                link(v.tensor_scalar(slot[:, 2, :], slot[:, 0, :], SLOTS - 0.5, None, ALU.is_gt))
                link(v.scalar_tensor_tensor(slot[:, 0, :], slot[:, 1, :], float(SLOTS), slot[:, 0, :], ALU.mult, ALU.add))
                link(v.tensor_scalar(slot[:, 1, :], slot[:, 1, :], -float(SLOTS), float((GROUPS - 1) * SLOTS),
                                     ALU.mult, ALU.add))
                link(v.tensor_tensor(slot[:, 1, :], slot[:, 1, :], slot[:, 2, :], ALU.mult))
                link(v.tensor_tensor(slot[:, 0, :], slot[:, 0, :], slot[:, 1, :], ALU.add))
                for t in range(NT):
                    v.tensor_scalar(sel_slots[:, t, :], iota[:], slot[:, 0, t:t + 1], None, ALU.is_equal)\
                        .then_inc(sem(f"slots{l}"), 1)
                link(v.tensor_scalar(over[:, 0, :], r[:, 2 * GROUPS:3 * GROUPS], SLOTS + 0.5, None, ALU.is_gt))
                v.tensor_reduce(over[:, 1, 0:1], over[:, 0, :], AX, ALU.max)
                link(v.tensor_tensor(over[:, 0, :], over[:, 0, :], index_g[:], ALU.mult))
                link(v.tensor_reduce(over[:, 1, 1:2], over[:, 0, :], AX, ALU.max))
                v.tensor_copy(over_group[l][0:1, :], over[0:1, 1, 0:2]).then_inc(sem(f"over_known{l}"), 1)
                free(v.tensor_copy(over[:, 0, :], r[:, 2 * GROUPS:3 * GROUPS]), ("rank", l))
                for c in range(1, KD, 2):
                    ready(dve, ("gather", l, c))
                    free(v.tensor_copy(xg_all[:, c, 0:HALF], bank(("gather", l, c))[:]), ("gather", l, c))
                ready(dve, ("gather_over", l, 1))
                free(v.tensor_copy(xg_all[:, 4:8, HALF:], bank(("gather_over", l, 1))[:].rearrange("p (c n) -> p c n", c=4)),
                     ("gather_over", l, 1))
                ready(dve, ("slotsT", l, 1))
                free(v.tensor_copy(slots_T[:, 2:4, :], bank(("slotsT", l, 1))[:].rearrange("p (c n) -> p c n", c=2)),
                     ("slotsT", l, 1))
                ready(dve, ("slotsT", l, 2))
                free(v.tensor_copy(slots_T[:, 4, :], bank(("slotsT", l, 2))[:, 0:T]), ("slotsT", l, 2))
                ready(dve, ("slot_gates", l))
                free(v.tensor_copy(slot_gates, bank(("slot_gates", l))[:, 0:STEPS * PER_GROUP]), ("slot_gates", l))
                freed(dve, ("slot_gates", l))

                def step(i):
                    for e in range(PER_GROUP):
                        freed(dve, ("gate", l, e), i)
                        ready(dve, ("up", l, e), i)
                        free(v.scalar_tensor_tensor(hx[:, e % 2, :], sg[:, e % 2, :],
                                                    slot_gates[:, bass.ds(i * PER_GROUP + e, 1)],
                                                    bank(("up", l, e))[:], ALU.mult, ALU.mult), ("up", l, e))
                    ready(dve, ("y", l, 1), i)
                    free(v.tensor_copy(y_sb[:, bass.ds(i, 1), HALF:].rearrange("p o n -> p (o n)"), bank(("y", l, 1))[:]),
                         ("y", l, 1))
                more = spilled(dve, l)
                with dve.Fori(0, GROUPS) as i:
                    step(i)
                with dve.If(more > 0):
                    step(GROUPS)
                with dve.Else():
                    v.memset(y_sb[:, GROUPS, :], 0.0).then_inc(sem(f"y_none{l}"), 1)
                    dve.wait_ge(sem(f"y_none{l}"), 1)
                    skipped(dve, bank_free, [("up", l, 2), ("up", l, 3), ("y", l, 1)])
                for t in range(NT):
                    for h in range(2):
                        ready(dve, ("scatter", l, t, h))
                        cols = slice(h * HALF, (h + 1) * HALF)
                        ins = v.scalar_tensor_tensor(res[:, t, cols], xtok[:, t, cols], ALPHA,
                                                     bank(("scatter", l, t, h))[:], ALU.mult, ALU.add)
                        free(ins, ("scatter", l, t, h))
                freed(dve, ("scatter", l, NT - 1, 1))

            freed(dve, ("pw2", 1, NT - 1))
            layer_norm("ln0")
            evac_T("ln0", xT, R_MIXG, R_MIXB)
            dve.wait_ge(sem("ln0_tok"), 2)
            dve.wait_ge(sem("biases"), 16)
            experts(0)
            layer_norm("ln1")
            evac_T("ln1", xT, R_FFNG, R_FFNB)
            dve.wait_ge(sem("par_gains"), 16 * 5)
            link(v.tensor_tensor(osq[:, 0:2 * HD].rearrange("p (a b) -> p a b", a=2), lamb[:, 0::2, :], lamb[:, 1::2, :],
                                 ALU.mult))
            v.tensor_reduce(lam[:, 0:2], osq[:, 0:2 * HD].rearrange("p (a b) -> p a b", a=2), AX, ALU.add)\
                .then_inc(sem("lam_dot"), 1)
            for name, dst in (("k", kT), ("q", qT)):
                for n in range(1, KD, 2):
                    ready(dve, (name, n))
                    free(v.tensor_copy(dst[:, n, :], bank((name, n))[:, 0:T]), (name, n))
            for half in range(2):
                ready(dve, ("v", half, 1))
                free(v.tensor_copy(vtok[:, 1, half * HALF:(half + 1) * HALF], bank(("v", half, 1))[:]), ("v", half, 1))
            dve.wait_ge(sem("lam_exp"), 1)
            link(v.tensor_tensor(lam[:, 4:5], lam[:, 2:3], lam[:, 3:4], ALU.subtract))
            link(v.tensor_scalar(lam[:, 5:6], lam[:, 4:5], LAMBDA_INIT, None, ALU.add))
            dve.wait_ge(sem("bias1"), 16)

            def logits(u):
                qt, h = units[u]
                n = (qt + 1) * P
                ready(dve, ("s", u))
                b = bank(("s", u))[:].rearrange("p (m k) -> p m k", m=2)[:, :, 0:n]
                free(v.scalar_tensor_tensor(logit[:, u % 2, :, 0:n], b, HD ** -0.5,
                                            bcast(bias1[:, h:h + 1, P - qt * P:T], 2, n), ALU.mult, ALU.add), ("s", u))
                freed(dve, ("s", u))
                v.tensor_reduce(dneg[:, u % 2, :], logit[:, u % 2, :, 0:n], AX, ALU.max, negate=True)\
                    .then_inc(sem("dmax"), 1)

            def difference(u):
                qt, h = units[u]
                n = (qt + 1) * P
                dve.wait_ge(sem("dexp"), 2 * (u + 1))
                link(v.reciprocal(dinv[:, u % 2, :], dsum[:, u % 2, :]))
                link(v.tensor_scalar(prob[:, u % 2, 1, 0:n], prob[:, u % 2, 1, 0:n], dinv[:, u % 2, 1:2], lam[:, 5:6],
                                     ALU.mult, ALU.mult))
                if u >= 2:
                    ready(dve, ("pT", u - 2))
                v.scalar_tensor_tensor(diffp[:, u % 2, 0:n], prob[:, u % 2, 0, 0:n], dinv[:, u % 2, 0:1],
                                       prob[:, u % 2, 1, 0:n], ALU.mult, ALU.subtract).then_inc(sem("diffp"), 1)

            def heads_out(qt, b):
                ready(dve, ("o", qt, b))
                free(v.tensor_copy(otok[:, qt, b * HALF:(b + 1) * HALF], bank(("o", qt, b))[:]), ("o", qt, b))
            logits(0)
            for u in range(len(units)):
                if u + 1 < len(units):
                    logits(u + 1)
                difference(u)
                if u % 4 == 0 and u:
                    heads_out((u // 4 - 1) // 2, (u // 4 - 1) % 2)
            heads_out(1, 1)
            freed(dve, ("o", 1, 1))
            for t in range(NT):
                link(v.tensor_tensor(osq, otok[:, t, :], otok[:, t, :], ALU.mult))
                v.tensor_reduce(oms[:, t, :], osq.rearrange("p (h d) -> p h d", h=HEADS), AX, ALU.add)\
                    .then_inc(sem("oms"), 1)
                dve.wait_ge(sem("oms"), t + 1)
            for t in range(NT):
                dve.wait_ge(sem("ostd"), t + 1)
                o = otok[:, t, :].rearrange("p (h d) -> p h d", h=HEADS)
                link(v.reciprocal(oms[:, t, :], ostd[:, t, :]))
                link(v.tensor_tensor(o, o, bcast(oms[:, t, :].unsqueeze(2), HEADS, VD), ALU.mult))
                v.scalar_tensor_tensor(o, o, 1.0 - LAMBDA_INIT, bcast(subg[:].unsqueeze(1), HEADS, VD),
                                       ALU.mult, ALU.mult).then_inc(sem("onorm"), 1)
            evac_T("o", xT)
            dve.wait_ge(sem("ln1_tok"), 2)
            for half in range(2):
                for t in range(NT):
                    cols = slice(half * HALF, (half + 1) * HALF)
                    ready(dve, ("wo", half, t))
                    free(v.scalar_tensor_tensor(res[:, t, cols], xtok[:, t, cols], ALPHA, bank(("wo", half, t))[:],
                                                ALU.mult, ALU.add), ("wo", half, t))
            freed(dve, ("wo", 1, NT - 1))
            layer_norm("ln2")
            evac_T("ln2", xT, R_MIXG + KD, R_MIXB + KD)
            dve.wait_ge(sem("ln2_tok"), 2)
            experts(1)
            layer_norm("ln3")

            dve.wait_ge(sem("rows3"), 32)
            for t in range(NT):
                dve.wait_ge(sem("ln3_xhat"), t + 1)
                link(v.tensor_tensor(xtok[:, t, :], res[:, t, :], rows[1][:, 0, :], ALU.mult))
                v.tensor_tensor(xtok[:, t, :], xtok[:, t, :], rows[1][:, 1, :], ALU.add).then_inc(sem("ln3_tok"), 1)
            rms_norm("rm0")
            evac_T("rm0", xT, R_MIX2)
            for t in range(NT):
                ready(dve, ("ikw", t))
                free(v.tensor_copy(ikw[:, t, :], bank(("ikw", t))[:, 0:IKW]), ("ikw", t))
            freed(dve, ("ikw", NT - 1))
            v.tensor_scalar(iws, ikw[:, :, HD:HD + IDX_HEADS], IDX_HEADS ** -0.5 * HD ** -0.5, None, ALU.mult)
            v.tensor_copy(ikd[:, :, 0:HD], ikw[:, :, 0:HD])
            link(v.tensor_copy(ikd[:, :, HD:], ikw[:, :, 0:HD]))
            for t in range(NT):
                ready(dve, ("aq", t))
                free(v.tensor_copy(aq[:, t, :], bank(("aq", t))[:]), ("aq", t))
            for t in range(NT):
                freed(dve, ("aq", t))
                freed(dve, ("akv", t))
                link(v.tensor_tensor(asq, aq[:, t, :], aq[:, t, :], ALU.mult))
                link(v.tensor_reduce(qkms[:, t, 0:8], asq.rearrange("p (h d) -> p h d", h=8), AX, ALU.add))
                link(v.tensor_tensor(asq[:, 0:P], akv[:, t, 0:P], akv[:, t, 0:P], ALU.mult))
                ins = v.tensor_reduce(qkms[:, t, 8:10], asq[:, 0:P].rearrange("p (h d) -> p h d", h=2), AX, ALU.add)
                if t == 0:
                    link(ins)
            ins.then_inc(sem("qk_ms"), 1)
            dve.wait_ge(sem("qk_std"), 1)
            link(v.reciprocal(qkms, qkstd))
            for t in range(NT):
                o = aq[:, t, :].rearrange("p (h d) -> p h d", h=8)
                link(v.tensor_tensor(o, o, bcast(qkms[:, t, 0:8].unsqueeze(2), 8, HD), ALU.mult))
                link(v.tensor_tensor(o, o, bcast(qg[:].unsqueeze(1), 8, HD), ALU.mult))
                o = akv[:, t, 0:P].rearrange("p (h d) -> p h d", h=2)
                link(v.tensor_tensor(o, o, bcast(qkms[:, t, 8:10].unsqueeze(2), 2, HD), ALU.mult))
                for twice in range(2):
                    ins = v.tensor_tensor(kd[:, t, :, twice * HD:(twice + 1) * HD], o, bcast(kg[:].unsqueeze(1), 2, HD),
                                          ALU.mult)
            ins.then_inc(sem("qk_norm"), 1)
            for t in (1,):
                ready(dve, ("hi", t))
                free(v.tensor_copy(itok[:, t, :], bank(("hi", t))[:]), ("hi", t))
            ready(dve, ("qaT", 1))
            free(v.tensor_copy(qaT[:, 2:4, :], bank(("qaT", 1))[:].rearrange("p (c t) -> p c t", c=2)), ("qaT", 1))
            ready(dve, "iqT")
            free(v.tensor_copy(iqT, bank("iqT")[:].rearrange("p (c t) -> p c t", c=2)), "iqT")
            dve.wait_ge(sem("hz"), 3)
            dve.wait_ge(sem("hk"), 1)
            link(v.scalar_tensor_tensor(zf, zf, 0.0, ez, ALU.min, ALU.subtract))
            dve.wait_ge(sem("reset"), 2)
            G = gcum.rearrange("p h t -> p (h t)")
            link(v.tensor_tensor_scan(G, reset.rearrange("p h t -> p (h t)"), zf.rearrange("p h t -> p (h t)"), 0.0,
                                      ALU.mult, ALU.add))
            for qt in range(NT):
                n = (qt + 1) * P
                for b in range(2):
                    freed(dve, ("is", qt, b))
                acc = iscore[:, qt, 0:n]
                link(v.tensor_scalar(acc, relus[:, 0, 0:n], iws[:, qt, 0:1], None, ALU.mult))
                for hh in range(1, IDX_HEADS):
                    ins = v.scalar_tensor_tensor(acc, relus[:, hh, 0:n], iws[:, qt, hh:hh + 1], acc, ALU.mult, ALU.add)
                    if hh < IDX_HEADS - 1:
                        link(ins)
                ins.then_inc(sem("isc"), 1)
            for n in range(4):
                ready(dve, ("ch", n))
                free(v.tensor_copy(ch[:, n, :], bank(("ch", n))[:, 0:T]), ("ch", n))
            for qt in range(NT):
                n = (qt + 1) * P
                dve.wait_ge(sem("causal"), qt + 1)
                sc = iscore[:, qt, 0:n]
                for r in range(TOPK // 8):
                    link(v.max(top8, sc))
                    link(v.match_replace(sc, top8, sc, TAKEN))
                v.tensor_scalar(sc, sc, TAKEN / 2, MASKED, ALU.is_gt, ALU.mult).then_inc(sem("chosen"), 1)
            for b in range(4):
                freed(dve, ("cc", b))
                freed(dve, ("ch", b))
                freed(dve, ("cb", b))
            dve.wait_ge(sem("upad0"), 1)
            link(v.tensor_tensor(upad[:, :, 2:], cc, ch, ALU.mult))
            for c in range(4):
                tap = [pcol[:, R_CW2 + j * 4 + c:R_CW2 + j * 4 + c + 1] for j in range(3)]
                link(v.tensor_scalar(ycT[:, c, :], upad[:, c, 0:T], tap[0], None, ALU.mult))
                for j in (1, 2):
                    link(v.scalar_tensor_tensor(ycT[:, c, :], upad[:, c, j:j + T], tap[j], ycT[:, c, :], ALU.mult, ALU.add))
            v.tensor_tensor(ycT, ycT, cb, ALU.mult).then_inc(sem("yc"), 1)

            def logits2(k):
                qt, u = k // 4, k % 4
                n = (qt + 1) * P
                if u == 0:
                    dve.wait_ge(sem("mb"), qt + 1)
                ready(dve, ("s2", qt, u))
                if k >= 2:
                    ready(dve, ("p2T", (k - 2) // 4, (k - 2) % 4, 1))
                b = bank(("s2", qt, u))[:].rearrange("p (m k) -> p m k", m=2)[:, :, 0:n]
                free(v.scalar_tensor_tensor(s2[:, u % 2, :, 0:n], b, HD ** -0.5, mb[qt][:, unit_heads(u)[0]:unit_heads(u)[1] + 1:2, :],
                                            ALU.mult, ALU.add), ("s2", qt, u))
                freed(dve, ("s2", qt, u))
                v.tensor_reduce(aneg[:, u % 2, :], s2[:, u % 2, :, 0:n], AX, ALU.max, negate=True)\
                    .then_inc(sem("amax"), 1)

            def heads2_out(qt):
                dve.wait_ge(sem("aexp"), 8 * (qt + 1))
                link(v.reciprocal(ainv[:, qt, :], asum[:, qt, :]))
                ready(dve, ("o2", qt))
                free(v.tensor_tensor(yat[:, qt, :].rearrange("p (h d) -> p h d", h=HEADS),
                                     bank(("o2", qt))[:].rearrange("p (h d) -> p h d", h=HEADS),
                                     bcast(ainv[:, qt, :].unsqueeze(2), HEADS, HD), ALU.mult), ("o2", qt))
            logits2(0)
            for k in range(8):
                if k + 1 < 8:
                    logits2(k + 1)
                qt, u = k // 4, k % 4
                ready(dve, ("p2T", qt, u, 1))
                free(v.tensor_copy(pT2[:, 1, 0:qt + 1, :],
                                   bank(("p2T", qt, u, 1))[:, 0:(qt + 1) * P].rearrange("p (k n) -> p k n", n=P)),
                     ("p2T", qt, u, 1))
                if k == 4:
                    heads2_out(0)
            heads2_out(1)
            ready(dve, ("yaT", 1))
            free(v.tensor_copy(yaT[:, 2:4, :], bank(("yaT", 1))[:].rearrange("p (c t) -> p c t", c=2)), ("yaT", 1))

            freed(dve, ("hq", 3))
            link(v.tensor_copy(ke[:, :, 0:1], reset[:, :, 0:1]))
            v.tensor_copy(cstd[:, 0, 0:1], eps_ln[:]).then_inc(sem("hqk"), 1)

            def masked_in(n):
                for t in range(NT):
                    m = ident[:] if n == 0 else blockmask[:, n - 1, :]
                    m = bcast(m.unsqueeze(1), HH, P)
                    ready(dve, ("lev", n, t))
                    src = bank(("lev", n, t))[:].rearrange("p (h t) -> p h t", h=HH)
                    free(v.tensor_tensor(attT[:, t] if n == 0 else masked, src, m, ALU.mult), ("lev", n, t))
                    freed(dve, ("lev", n, t))
                    if n:
                        ins = v.tensor_tensor(attT[:, t], attT[:, t], masked, ALU.add)
                        if n == len(LEVELS):
                            ins.then_inc(sem("att"), 1)
                            dve.wait_ge(sem("att"), t + 1)
                        else:
                            link(ins)

            def decayed(n, b):
                half = b // 2
                view = lambda x: x.rearrange("p h t -> p (h t)").rearrange("p (c b) -> p c b", b=b)
                g_, e_ = view(gcum), view(ez)
                mid = bcast(g_[:, :, half - 1:half], HH * T // b, half)
                v.tensor_tensor(e_[:, :, 0:half], mid, g_[:, :, 0:half], ALU.subtract)
                if b > CHUNK:
                    ins = v.tensor_copy(e_[:, :, half:], g_[:, :, half:])
                else:
                    ins = v.tensor_tensor(e_[:, :, half:], g_[:, :, half:], mid, ALU.subtract)
                ins.then_inc(sem("hdiff"), 1)
                if b == 2 * CHUNK:
                    dve.wait_ge(sem("hdiff"), n)
                    link(v.tensor_tensor(g_[:, :, half:], g_[:, :, half:], mid, ALU.add))
                dve.wait_ge(sem("hdecay"), n)
                v.tensor_tensor(view(qe)[:, :, half:], view(qh)[:, :, half:], e_[:, :, half:], ALU.mult)
                v.tensor_tensor(view(ke)[:, :, 0:half], view(kk)[:, :, 0:half], e_[:, :, 0:half], ALU.mult)\
                    .then_inc(sem("hqk"), 1)
            for n, b in enumerate(LEVELS):
                if n:
                    ready(dve, ("lev", n, NT - 1))
                decayed(n + 1, b)
                masked_in(n)
            ready(dve, ("lev", len(LEVELS), NT - 1))
            decayed(len(LEVELS) + 1, T)
            masked_in(len(LEVELS))
            for t in range(NT):
                ready(dve, ("oh", t))
                free(v.tensor_copy(yh[:, t, :], bank(("oh", t))[:]), ("oh", t))
                freed(dve, ("oh", t))
                y = yh[:, t, :].rearrange("p (h d) -> p h d", h=HH)
                link(v.tensor_tensor(masked, y, y, ALU.mult))
                v.tensor_reduce(hms[:, t, :], masked, AX, ALU.add).then_inc(sem("hms"), 1)
                dve.wait_ge(sem("hms"), t + 1)
            for t in range(NT):
                y = yh[:, t, :].rearrange("p (h d) -> p h d", h=HH)
                dve.wait_ge(sem("hstd"), t + 1)
                link(v.reciprocal(hms[:, t, :], hstd[:, t, :]))
                link(v.tensor_tensor(y, y, bcast(hms[:, t, :].unsqueeze(2), HH, VD), ALU.mult))
                link(v.tensor_tensor(y, y, bcast(hng[:].unsqueeze(1), HH, VD), ALU.mult))
                freed(dve, ("hg", t))
                v.tensor_tensor(yh[:, t, :], yh[:, t, :], hgs[:, t, :], ALU.mult).then_inc(sem("yh"), 1)
            ready(dve, ("yhT", 1))
            free(v.tensor_copy(yhT[:, 2:4, :], bank(("yhT", 1))[:].rearrange("p (c t) -> p c t", c=2)), ("yhT", 1))
            for br in range(3):
                for t in range(NT):
                    for h in range(2):
                        g_ = gates[:, 2 * br + h, t, :]
                        m = mixed[:, t, h * HALF:(h + 1) * HALF]
                        ready(dve, ("branch", br, t, h))
                        freed(dve, ("gates", 2 * br + h, t))
                        free(v.tensor_tensor(g_ if br else m, g_, bank(("branch", br, t, h))[:], ALU.mult),
                             ("branch", br, t, h))
                        if br:
                            freed(dve, ("branch", br, t, h))
                            ins = v.tensor_tensor(m, m, g_, ALU.add)
                            if (br, t, h) == (2, NT - 1, 1):
                                ins.then_inc(sem("mixed"), 1)
                            else:
                                link(ins)
            evac_T("mixed", xT)
            for h in range(2):
                for t in range(NT):
                    x = xtok[:, t, h * HALF:(h + 1) * HALF]
                    ready(dve, ("out", h, t))
                    free(v.tensor_tensor(x, x, bank(("out", h, t))[:], ALU.add), ("out", h, t))
                    if h:
                        freed(dve, ("out", h, t))
                        v.tensor_copy(cstd[:, 0, 0:1], eps_ln[:]).then_inc(sem("mixed_in"), 1)
            rms_norm("rm1")
            evac_T("rm1", xT, R_MLP2)

            def mlp(i):
                for j in range(2):
                    for t in range(NT):
                        freed(dve, ("mu", j, t), i)
                        v.tensor_tensor(mh[:, j, t, :], mr[:, j, t, :], mr[:, j, t, :], ALU.mult).then_inc(sem("mh"), 1)
                    ready(dve, ("mT", j, 1), i)
                    free(v.tensor_copy(mhT[:, j, :, P:], bank(("mT", j, 1))[:].rearrange("p (c n) -> p c n", c=4)),
                         ("mT", j, 1))
            with dve.Fori(0, 4) as i:
                mlp(i)
            dve.wait_ge(sem("md_read"), 8)
            for t in range(NT):
                for h in range(2):
                    cols = slice(h * HALF, (h + 1) * HALF)
                    ins = v.tensor_tensor(res[:, t, cols], xtok[:, t, cols], bank(("md", t, h))[:], ALU.add)
                ins.then_inc(sem("result"), 1)


_INS = ["x", "a_w_pw1", "a_b_pw1", "a_w_dw", "a_b_dw", "a_ln_g", "a_ln_b", "a_w_pw2", "a_b_pw2", "w_kv", "b_w_q",
        "b_lambda", "b_subln_g", "b_w_o", "rel_bias", "ln_mix_g", "ln_mix_b", "ln_ffn_g", "ln_ffn_b", "router_w",
        "router_bias", "moe_w_gate", "moe_w_up", "moe_w_down", "rel_bias_2", "ln_mix_g_2", "w_in_2", "q_norm_g_2",
        "k_norm_g_2", "hgrn_norm_g_2", "conv_w_2", "w_up_attn_2", "w_up_hgrn_2", "w_up_conv_2", "w_out_2",
        "ln_mlp_g_2", "w_mlp_up_2", "w_mlp_down_2"]


def bucket_onehot():
    import numpy as np
    n_buckets, exact, far = 32, 16, 128
    dist = (T - 1) - np.arange(BIAS_LINE)
    near = np.maximum(dist, 1).astype(np.float32)
    large = exact + (np.log(near / np.float32(exact)) / np.float32(math.log(far / exact))
                     * np.float32(n_buckets - exact)).astype(np.int32)
    bucket = np.where(dist < exact, dist, np.minimum(large, n_buckets - 1))
    rows = np.arange(n_buckets + 1)[:, None]
    return np.where(dist >= 0, rows == bucket, rows == n_buckets).astype(np.float32)


def kernel(**inputs):
    import numpy as _np
    import concourse.bacc as _bacc
    from concourse import mybir as _mybir
    from concourse.bass_utils import run_bass_kernel_spmd as _run

    nc = _bacc.Bacc("TRN2", target_bir_lowering=False, num_devices=1)
    arrays, args = {}, {}
    for name in _INS + ["bucket_onehot"]:
        x = bucket_onehot() if name == "bucket_onehot" else _np.ascontiguousarray(inputs[name])
        arrays[f"in_{name}_dram"] = x
        args[name] = nc.dram_tensor(f"in_{name}_dram", x.shape, _mybir.dt.from_np(x.dtype), kind="ExternalInput").ap()
    out = nc.dram_tensor("out_0_dram", (1, T, D), F32, kind="ExternalOutput").ap()
    program(nc, args, out)
    r = _run(nc, [arrays], core_ids=[0])
    return r.results[0]["out_0_dram"]
```
